# Optimizing a Trainium2 kernel written in Bass

```python
import math
import jax, jax.numpy as jnp
from jax import lax
import numpy as np

D_MODEL = 2048
BATCH = 1
SEQ = 512
DEPTH = 1

MEM_LEN = 256
N_HEADS_A = 8
N_KV_A = 2
HEAD_DIM_A = 128
ATTN_WIDTH = N_HEADS_A * HEAD_DIM_A
KV_WIDTH = N_KV_A * HEAD_DIM_A
IDX_HEADS = 16
IDX_DIM = 64
TOPK_MAX = 256
BLOCK_Q = 128
REL_BUCKETS = 32
REL_MAX_DIST = 128
SSM_WIDTH = D_MODEL // 4
SSM_GROUP = 16
SSM_GROUPS = SSM_WIDTH // SSM_GROUP
SSM_STATE = 64
X_HEADS = 4
X_HEAD_DIM = 128
X_WIDTH = X_HEADS * X_HEAD_DIM
D_FF = (11 * D_MODEL) // 4
CONV_WIDTH = 3
EPS = 1e-6
IN_SPLITS = (ATTN_WIDTH, KV_WIDTH, KV_WIDTH, IDX_HEADS * IDX_DIM, IDX_DIM, IDX_HEADS, SSM_WIDTH, D_MODEL, D_MODEL)
IN_COLS = sum(IN_SPLITS)

kernel_name = "hybrid_dsa_s5_gated_block"

def rms_norm(x, g):
    xf = x.astype(jnp.float32)
    y = xf * lax.rsqrt(jnp.mean(xf * xf, axis=-1, keepdims=True) + EPS)
    return (y * g.astype(jnp.float32)).astype(x.dtype)

def t5_bucket(n):
    n = jnp.maximum(n, 0)
    max_exact = REL_BUCKETS // 2
    nf = jnp.maximum(n, 1).astype(jnp.float32)
    large = max_exact + (jnp.log(nf / max_exact) / math.log(REL_MAX_DIST / max_exact)
                         * (REL_BUCKETS - max_exact)).astype(jnp.int32)
    large = jnp.minimum(large, REL_BUCKETS - 1)
    return jnp.where(n < max_exact, n, large)

def sparse_attention(q, k, v, qi, ki, wi, rel_bias):
    B, S = q.shape[0], q.shape[1]
    nb = S // BLOCK_Q
    k_sel = min(TOPK_MAX, S // 4)
    grp = N_HEADS_A // N_KV_A
    scale = HEAD_DIM_A ** -0.5
    neg = jnp.finfo(jnp.float32).min
    key_pos = jnp.arange(S, dtype=jnp.int32)

    def to_blocks(a):
        return jnp.moveaxis(a.reshape((B, nb, BLOCK_Q) + a.shape[2:]), 1, 0)

    starts = jnp.arange(nb, dtype=jnp.int32) * BLOCK_Q

    def one_block(args):
        qb, qib, wib, start = args
        q_pos = start + jnp.arange(BLOCK_Q, dtype=jnp.int32)
        causal = key_pos[None, :] <= q_pos[:, None]
        dots = jnp.einsum('bqhd,bsd->bqhs', qib, ki)
        idx_score = jnp.einsum('bqh,bqhs->bqs', wib, jax.nn.relu(dots)).astype(jnp.float32)
        idx_score = jnp.where(causal[None], idx_score, -jnp.inf)
        _, sel = lax.top_k(idx_score, k_sel)
        k_g = jax.vmap(lambda kk, ii: kk[ii])(k, sel)
        v_g = jax.vmap(lambda vv, ii: vv[ii])(v, sel)
        qg = qb.reshape(B, BLOCK_Q, N_KV_A, grp, HEAD_DIM_A)
        logits = jnp.einsum('bqhgd,bqnhd->bqhgn', qg, k_g).astype(jnp.float32) * scale
        dist = q_pos[None, :, None] - sel
        bias = rel_bias[t5_bucket(dist)].astype(jnp.float32)
        bias = bias.reshape(B, BLOCK_Q, k_sel, N_KV_A, grp).transpose(0, 1, 3, 4, 2)
        valid = (dist >= 0)[:, :, None, None, :]
        logits = jnp.where(valid, logits + bias, neg)
        p = jax.nn.softmax(logits, axis=-1).astype(v.dtype)
        out = jnp.einsum('bqhgn,bqnhd->bqhgd', p, v_g)
        return out.reshape(B, BLOCK_Q, ATTN_WIDTH)

    outs = lax.map(one_block, (to_blocks(q), to_blocks(qi), to_blocks(wi), starts))
    return jnp.moveaxis(outs, 0, 1).reshape(B, S, ATTN_WIDTH)

def s5_branch(u, lam_re, lam_im, log_dt, b_re, b_im, c_re, c_im, d_skip, w_glu, b_glu):
    B, S, _ = u.shape
    ug = u.reshape(B, S, SSM_GROUPS, SSM_GROUP).astype(jnp.float32)
    dt = jnp.exp(log_dt.astype(jnp.float32))[:, None]
    lr = lam_re.astype(jnp.float32)
    li = lam_im.astype(jnp.float32)
    mag = jnp.exp(lr * dt)
    ar = mag * jnp.cos(li * dt)
    ai = mag * jnp.sin(li * dt)
    den = lr * lr + li * li
    nr = ar - 1.0
    coef_r = (nr * lr + ai * li) / den
    coef_i = (ai * lr - nr * li) / den
    br = b_re.astype(jnp.float32)
    bi = b_im.astype(jnp.float32)
    bbar_re = coef_r[..., None] * br - coef_i[..., None] * bi
    bbar_im = coef_r[..., None] * bi + coef_i[..., None] * br
    bu_re = jnp.einsum('bsgc,gpc->bsgp', ug, bbar_re)
    bu_im = jnp.einsum('bsgc,gpc->bsgp', ug, bbar_im)
    a_re = jnp.broadcast_to(ar, bu_re.shape)
    a_im = jnp.broadcast_to(ai, bu_im.shape)

    def combine(left, right):
        a1r, a1i, b1r, b1i = left
        a2r, a2i, b2r, b2i = right
        return (a2r * a1r - a2i * a1i,
                a2r * a1i + a2i * a1r,
                a2r * b1r - a2i * b1i + b2r,
                a2r * b1i + a2i * b1r + b2i)

    _, _, xr, xi = lax.associative_scan(combine, (a_re, a_im, bu_re, bu_im), axis=1)
    y = (jnp.einsum('bsgp,gcp->bsgc', xr, c_re.astype(jnp.float32))
         - jnp.einsum('bsgp,gcp->bsgc', xi, c_im.astype(jnp.float32))
         + d_skip.astype(jnp.float32) * ug)
    y = y.reshape(B, S, SSM_WIDTH).astype(u.dtype)
    g = jax.nn.gelu(y)
    return g * jax.nn.sigmoid(g @ w_glu + b_glu)

def cross_attention(h, mem_n, wq, wkv, wo):
    B, S, _ = h.shape
    M = mem_n.shape[1]
    q = (h @ wq).reshape(B, S, X_HEADS, X_HEAD_DIM)
    k, v = jnp.split(mem_n @ wkv, 2, axis=-1)
    k = k.reshape(B, M, X_HEADS, X_HEAD_DIM)
    v = v.reshape(B, M, X_HEADS, X_HEAD_DIM)
    logits = jnp.einsum('bshd,bmhd->bhsm', q, k).astype(jnp.float32) * (X_HEAD_DIM ** -0.5)
    p = jax.nn.softmax(logits, axis=-1).astype(v.dtype)
    out = jnp.einsum('bhsm,bmhd->bshd', p, v).reshape(B, S, X_WIDTH)
    return out @ wo

def conv_ffn(u, w_up, conv_w, conv_b, w_down):
    hdn = u @ w_up
    c = hdn.shape[-1]
    hdn = lax.conv_general_dilated(hdn, conv_w[:, None, :].astype(hdn.dtype), window_strides=(1,),
                                   padding=[(CONV_WIDTH - 1, 0)],
                                   dimension_numbers=('NWC', 'WIO', 'NWC'),
                                   feature_group_count=c) + conv_b
    a, b = jnp.split(hdn, 2, axis=-1)
    return (jax.nn.silu(a) * b) @ w_down

def setup_inputs(seed: int = 0) -> dict:
    key = jax.random.key(seed)
    ks = jax.random.split(key, 32)
    L = DEPTH
    f32 = jnp.float32

    def nrm(k, shape, scale):
        return jax.random.normal(k, shape, f32) * scale

    def gain(k, shape):
        return 1.0 + 0.02 * jax.random.normal(k, shape, f32)

    lam_re = -0.5 + 0.01 * jax.random.normal(ks[5], (L, SSM_GROUPS, SSM_STATE), f32)
    lam_im = (math.pi * jnp.arange(SSM_STATE, dtype=f32))[None, None, :] \
        + 0.01 * jax.random.normal(ks[6], (L, SSM_GROUPS, SSM_STATE), f32)
    uu = jax.random.uniform(ks[7], (L, SSM_GROUPS), f32)
    log_dt = math.log(1e-3) + uu * (math.log(1e-1) - math.log(1e-3))
    return {
        'x': nrm(ks[0], (BATCH, SEQ, D_MODEL), 1.0),
        'mem': nrm(ks[1], (BATCH, MEM_LEN, D_MODEL), 1.0),
        'rel_bias': nrm(ks[2], (REL_BUCKETS, N_HEADS_A), 0.1),
        'norm_mix': gain(ks[3], (L, D_MODEL)),
        'w_in': nrm(ks[4], (L, D_MODEL, IN_COLS), D_MODEL ** -0.5),
        'ssm_lambda_re': lam_re,
        'ssm_lambda_im': lam_im,
        'ssm_log_dt': log_dt,
        'ssm_b_re': nrm(ks[8], (L, SSM_GROUPS, SSM_STATE, SSM_GROUP), (2 * SSM_GROUP) ** -0.5),
        'ssm_b_im': nrm(ks[9], (L, SSM_GROUPS, SSM_STATE, SSM_GROUP), (2 * SSM_GROUP) ** -0.5),
        'ssm_c_re': nrm(ks[10], (L, SSM_GROUPS, SSM_GROUP, SSM_STATE), (2 * SSM_STATE) ** -0.5),
        'ssm_c_im': nrm(ks[11], (L, SSM_GROUPS, SSM_GROUP, SSM_STATE), (2 * SSM_STATE) ** -0.5),
        'ssm_d': nrm(ks[12], (L, SSM_GROUPS, SSM_GROUP), 1.0),
        'ssm_w_glu': nrm(ks[13], (L, SSM_WIDTH, SSM_WIDTH), SSM_WIDTH ** -0.5),
        'ssm_b_glu': nrm(ks[14], (L, SSM_WIDTH), 0.02),
        'w_branch_a': nrm(ks[15], (L, ATTN_WIDTH, D_MODEL), ATTN_WIDTH ** -0.5),
        'w_branch_b': nrm(ks[16], (L, SSM_WIDTH, D_MODEL), SSM_WIDTH ** -0.5),
        'w_out': nrm(ks[17], (L, D_MODEL, D_MODEL), D_MODEL ** -0.5),
        'norm_cross': gain(ks[18], (L, D_MODEL)),
        'norm_mem': gain(ks[19], (L, D_MODEL)),
        'w_cross_q': nrm(ks[20], (L, D_MODEL, X_WIDTH), D_MODEL ** -0.5),
        'w_cross_kv': nrm(ks[21], (L, D_MODEL, 2 * X_WIDTH), D_MODEL ** -0.5),
        'w_cross_o': nrm(ks[22], (L, X_WIDTH, D_MODEL), X_WIDTH ** -0.5),
        'norm_ffn': gain(ks[23], (L, D_MODEL)),
        'w_up': nrm(ks[24], (L, D_MODEL, 2 * D_FF), D_MODEL ** -0.5),
        'ffn_conv_w': nrm(ks[25], (L, CONV_WIDTH, 2 * D_FF), CONV_WIDTH ** -0.5),
        'ffn_conv_b': nrm(ks[26], (L, 2 * D_FF), 0.02),
        'w_down': nrm(ks[27], (L, D_FF, D_MODEL), D_FF ** -0.5),
        'norm_final': gain(ks[28], (D_MODEL,)),
    }

def reference(x, mem, rel_bias, norm_mix, w_in, ssm_lambda_re, ssm_lambda_im, ssm_log_dt,
              ssm_b_re, ssm_b_im, ssm_c_re, ssm_c_im, ssm_d, ssm_w_glu, ssm_b_glu,
              w_branch_a, w_branch_b, w_out, norm_cross, norm_mem, w_cross_q, w_cross_kv,
              w_cross_o, norm_ffn, w_up, ffn_conv_w, ffn_conv_b, w_down, norm_final):
    B, S, _ = x.shape
    offsets = [int(o) for o in np.cumsum(IN_SPLITS)[:-1]]
    idx_w_scale = (IDX_HEADS * IDX_DIM) ** -0.5
    for l in range(DEPTH):
        u = rms_norm(x, norm_mix[l])
        q, k, v, qi, ki, wi, s_in, g_a, g_b = jnp.split(u @ w_in[l], offsets, axis=-1)
        y_a = sparse_attention(
            q.reshape(B, S, N_HEADS_A, HEAD_DIM_A),
            k.reshape(B, S, N_KV_A, HEAD_DIM_A),
            v.reshape(B, S, N_KV_A, HEAD_DIM_A),
            qi.reshape(B, S, IDX_HEADS, IDX_DIM), ki, wi * idx_w_scale, rel_bias)
        y_b = s5_branch(s_in, ssm_lambda_re[l], ssm_lambda_im[l], ssm_log_dt[l], ssm_b_re[l],
                        ssm_b_im[l], ssm_c_re[l], ssm_c_im[l], ssm_d[l], ssm_w_glu[l], ssm_b_glu[l])
        z = jax.nn.sigmoid(g_a) * (y_a @ w_branch_a[l]) + jax.nn.sigmoid(g_b) * (y_b @ w_branch_b[l])
        x = x + z @ w_out[l]
        x = x + cross_attention(rms_norm(x, norm_cross[l]), rms_norm(mem, norm_mem[l]),
                                w_cross_q[l], w_cross_kv[l], w_cross_o[l])
        x = x + conv_ffn(rms_norm(x, norm_ffn[l]), w_up[l], ffn_conv_w[l], ffn_conv_b[l], w_down[l])
    return rms_norm(x, norm_final)


_drawn_inputs = setup_inputs


def setup_inputs(seed=0):
    import zlib

    import numpy as np

    out = dict(_drawn_inputs(seed))
    spreads = {}
    factors = {'rel_bias': 6.751,
     'norm_mix': 4.491,
     'ssm_lambda_re': 64.0,
     'ssm_lambda_im': 36.664,
     'ssm_log_dt': 37.528,
     'ssm_b_re': 50.816,
     'ssm_b_im': 52.56,
     'ssm_c_re': 51.016,
     'ssm_c_im': 50.936,
     'ssm_b_glu': 8.0,
     'norm_cross': 8.0,
     'norm_mem': 8.0,
     'norm_ffn': 3.911,
     'ffn_conv_b': 4.023,
     'norm_final': 7.462}
    for name, (base, spread) in spreads.items():
        noise = np.random.default_rng([zlib.crc32(name.encode()), seed]).standard_normal(out[name].shape)
        drawn = base * np.exp(spread * noise) if base else spread * noise
        out[name] = __import__('jax').numpy.asarray(drawn.astype(out[name].dtype))
    for name, factor in factors.items():
        out[name] = (out[name] * factor).astype(out[name].dtype)
    return out
```

```python
from contextlib import ExitStack, contextmanager

import numpy as np

import concourse.bass as bass
from concourse import mybir

F32 = mybir.dt.float32
F32R = mybir.dt.float32r
ALU = mybir.AluOpType
ACT = mybir.ActivationFunctionType
AX_X = mybir.AxisListType.X

P = 128
D = 2048
T = 512
KD = D // P
QT = T // P
M = 256
MT = M // P
HEADS, KVH, DH = 8, 2, 128
IH, ID = 16, 64
TOPK = min(256, T // 4)
BUCKETS = 32
SSM = D // 4
SB = SSM // P
GROUPS, GC, GP = 32, 16, 64
ST = GROUPS * GP // P
TPB = ST // SB
XH = 4
DFF = 11 * D // 4
FB = DFF // P
CH = 4
NCH = FB // CH
EPS = 1e-6
NEG = -1.0e30
LOWEST = -3.0e38
UT = 4
RING = 4
QS = float(DH) ** -0.5
WSCALE = float(IH * ID) ** -0.5
TWO_PI = 6.283185307179586
C1 = 6.28125
C2 = float(np.float32(TWO_PI - C1))
ROUND = 12582912.0
GELU_C = 2.0 * (2.0 / np.pi) ** 0.5
FLO = 32
FHI = T // FLO

KEYS = [P * (t + 1) for t in range(QT)]
OFF = [sum(KEYS[:t]) for t in range(QT)]
KOFF = [sum(T - P * j for j in range(t)) for t in range(QT)]
PAIRS = sum(KEYS)

PARAMS = [("g_mix", KD), ("g_cross", KD), ("g_mem", KD), ("g_ffn", KD), ("g_final", KD),
          ("ident", P), ("causal", P), ("lam_re", ST), ("lam_im", ST), ("log_dt", ST),
          ("b_glu", SB), ("d_skip", SB), ("conv_b", 2 * FB), ("conv_w", 2 * FB * 3)]
PCOL = {}
_at = 0
for _name, _n in PARAMS:
    PCOL[_name] = (_at, _n)
    _at += _n
NPARAM = _at
SPAN = T + P
PI_IN = 3.1415925
N_SPLIT_BEFORE_Q = 1 + 8 + KVH
N_SPLIT_BEFORE_B = N_SPLIT_BEFORE_Q + HEADS + SB
N_SPLIT_BEFORE_XQ = N_SPLIT_BEFORE_B + XH
UNITS_BEFORE_OUT = (1 + 8 + 2 * KVH + SB + HEADS) * (KD // UT) + KD * (KD // UT + 2) + KD * (KD // UT) + SB + KD
FIRST_POOL_CUT = (1 + 8) * (KD // UT) + 4
LAST_POOL_CUT = UNITS_BEFORE_OUT + KD * (KD // UT) + 4 * XH + KD + 4 - 8

P_TILES = [m for m in range(KD) if m % 3 == 1]
V_TILES = [m for m in range(KD) if m % 3 != 1]

LAST_SQUARES = 4

EARLY = 3

FIRST_CUTS = (1, 2, 2, 1)

UNITS_D = KD // UT
N_UNITS = ((1 + 8 + 4 + 4 + 8) * UNITS_D + 16 * (UNITS_D + 2) + 16 * UNITS_D + SB + 16 + 16 * UNITS_D
           + 4 * UNITS_D + KD + 4 * UNITS_D + 16 + 2 * FB * UNITS_D + NCH * 16)


class Count:

    def __init__(self, const=0, terms=()):
        self.const, self.terms = const, tuple(terms)

    def plus(self, k):
        return Count(self.const + k, self.terms)

    def times(self, k):
        return Count(self.const * k, [(r, f * k) for r, f in self.terms])

    def value(self):
        v = self.const
        for register, factor in self.terms:
            v = register * factor + v
        return v


class Tally:

    def __init__(self, eng):
        self.eng, self.at = eng, {}

    def now(self, name):
        return self.at.setdefault(name, Count())

    def move(self, name, k=1):
        self.at[name] = self.now(name).plus(k)

    def value(self, name):
        return self.now(name).value()

    def next(self, name, k=1):
        self.move(name, k)
        return self.value(name)

    def due(self, name, k=1):
        self.move(name, k)
        c = self.now(name)
        assert c.const > 0 or not c.terms, name
        return c.const > 0

    def register(self, name):
        c = self.now(name)
        return self.eng.snap(self.eng.to_reg(c.value())) if c.terms else c.value()

    def add(self, name):
        self.move(name)
        return 1

    @contextmanager
    def loop(self, trips, **per):
        start = dict(self.at)
        with self.eng.Fori(0, trips) as i:
            for name, k in per.items():
                c = start.get(name, Count())
                self.at[name] = Count(c.const, c.terms + ((i, k),))
            yield i
            for name, c in self.at.items():
                moved = c.const - start.get(name, Count()).const
                assert moved == per.get(name, 0), (name, moved, per.get(name, 0))
        for name, k in per.items():
            self.at[name] = start.get(name, Count()).plus(k * trips)


def layer(nc, wstream, xt, memt, params, b_re, b_im, c_re, c_im, rel, onehot, strips, out):
    ctx = ExitStack()
    with ctx:
        def sb(name, shape, dt=F32, on=ctx):
            return on.enter_context(nc.sbuf_tensor(name, [P] + list(shape), dt))

        act_hi, act_lo = sb("act_hi", [KD, T], F32R), sb("act_lo", [KD, T], F32R)
        raw = sb("raw", [RING, T])
        whi, wlo = sb("whi", [RING, T], F32R), sb("wlo", [RING, T], F32R)
        par = sb("par", [NPARAM])
        ones = sb("ones", [P])
        rstd, sumsq = sb("rstd", [T]), sb("sumsq", [T])
        sq = sb("sq", [2, T])
        stage = sb("stage", [2, T])
        small = sb("small", [64])

        with ExitStack() as e:
            q_hi, q_lo = sb("q_hi", [T], F32R, e), sb("q_lo", [T], F32R, e)
            strip = sb("strip", [T], F32, e)
            biasm = sb("biasm", [PAIRS], F32, e)
            mask = sb("mask", [PAIRS], F32, e)
            widx = sb("widx", [QT, IH], F32, e)
            with ExitStack() as f:
                relu = sb("relu", [2, T], F32, f)
                score = sb("score", [PAIRS - P], F32, f)
                ki_hi, ki_lo = sb("ki_hi", [T], F32R, f), sb("ki_lo", [T], F32R, f)
            prob = sb("prob", [PAIRS], F32, e)
            pt_hi, pt_lo = sb("pt_hi", [PAIRS], F32R, e), sb("pt_lo", [PAIRS], F32R, e)
        res = sb("res", [KD, T])
        with ExitStack() as e:
            mem_acc, rmem, vmem = sb("mem_acc", [M], F32, e), sb("rmem", [M + MT], F32, e), sb("vmem", [M + MT], F32, e)
            kc_hi, kc_lo = sb("kc_hi", [XH, M], F32R, e), sb("kc_lo", [XH, M], F32R, e)
            vc_hi, vc_lo = sb("vc_hi", [MT, T], F32R, e), sb("vc_lo", [MT, T], F32R, e)
            with ExitStack() as f:
                mem_raw = sb("mem_raw", [KD, M], F32, f)
                mem_hi, mem_lo = sb("mem_hi", [KD, M], F32R, f), sb("mem_lo", [KD, M], F32R, f)
            with ExitStack() as f:
                xq_hi, xq_lo = sb("xq_hi", [T], F32R, f), sb("xq_lo", [T], F32R, f)
                xprob = sb("xprob", [QT, M], F32, f)
                xpt_hi, xpt_lo = sb("xpt_hi", [MT, T], F32R, f), sb("xpt_lo", [MT, T], F32R, f)
                oc_hi, oc_lo = sb("oc_hi", [XH, T], F32R, f), sb("oc_lo", [XH, T], F32R, f)
        with ExitStack() as e:
            h_hi, h_lo = sb("h_hi", [2 * CH, T], F32R, e), sb("h_lo", [2 * CH, T], F32R, e)
            padded = sb("padded", [2, T + 2], F32, e)
            conv = sb("conv", [2, T], F32, e)
            sigm = sb("sigm", [T], F32, e)
        with ExitStack() as e:
            qi_hi, qi_lo = sb("qi_hi", [8, T], F32R, e), sb("qi_lo", [8, T], F32R, e)
        with ExitStack() as e:
            work = sb("work", [PAIRS - P], F32, e)
            work2 = sb("work2", [T], F32, e)
        with ExitStack() as e:
            ya_hi, ya_lo = sb("ya_hi", [HEADS, T], F32R, e), sb("ya_lo", [HEADS, T], F32R, e)
        sig_b = sb("sig_b", [KD, T])
        s_in = sb("s_in", [SB, T])
        with ExitStack() as e:
            tab_c, tab_s = sb("tab_c", [ST, FLO], F32, e), sb("tab_s", [ST, FLO], F32, e)
            hop_c, hop_s = sb("hop_c", [ST, FHI], F32, e), sb("hop_s", [ST, FHI], F32, e)
            mag = sb("mag", [ST], F32, e)
            bbt_re, bbt_im = sb("bbt_re", [SB, P], F32, e), sb("bbt_im", [SB, P], F32, e)
            cc_re, cc_im = sb("cc_re", [ST, 2 * GC], F32, e), sb("cc_im", [ST, 2 * GC], F32, e)
            with ExitStack() as f:
                k_hi, k_lo = sb("k_hi", [KVH, T], F32R, f), sb("k_lo", [KVH, T], F32R, f)
                v_hi, v_lo = sb("v_hi", [QT, KVH * P], F32R, f), sb("v_lo", [QT, KVH * P], F32R, f)
            with ExitStack() as f:
                bb_re, bb_im = sb("bb_re", [ST * 32], F32, f), sb("bb_im", [ST * 32], F32, f)
                s5t = sb("s5t", [4, ST * 32], F32, f)
                s5p = sb("s5p", [24, ST], F32, f)
                s5q = sb("s5q", [ST * FLO // 2], F32, f)
                rel_sb, onehot_sb = sb("rel_sb", [HEADS], F32, f), sb("onehot_sb", [SPAN], F32, f)
            with ExitStack() as f:
                cost, sint = sb("cost", [T], F32, f), sb("sint", [T], F32, f)
                wr, wi = sb("wr", [T], F32, f), sb("wi", [T], F32, f)
                zr, zi = sb("zr", [T], F32, f), sb("zi", [T], F32, f)
                rot = sb("rot", [T], F32, f)
                u_now = sb("u_now", [T], F32, f)
                bb_now = sb("bb_now", [2, P], F32, f)
                c_now = sb("c_now", [2, TPB, 2 * GC], F32, f)
        with ExitStack() as e:
            g_hi, g_lo = sb("g_hi", [SB, T], F32R, e), sb("g_lo", [SB, T], F32R, e)
            yb_hi, yb_lo = sb("yb_hi", [SB, T], F32R, e), sb("yb_lo", [SB, T], F32R, e)

        bank = [ctx.enter_context(nc.psum_tensor(f"bank{i}", [P, T], F32)) for i in range(8)]
        proj, pair, turn, attn = bank[0:2], bank[2:4], bank[4:7], bank[7]
        down_bank = [bank[2], bank[3], bank[1], bank[0]]
        out_bank = [bank[1], bank[0], turn[2], bank[2]]

        sems = {}
        for names in ("raw0 raw1 raw2 raw3 w_hi w_lo units_done proj_read",
                      "params_in strip_out strip_in dup_in out_stored s5_in",
                      "act_hi_done act_lo_done ones_set square_done square_read sumsq_total inverse_done",
                      "root_done hi_done lo_done dve_step pool_step wi_turned",
                      "dots_done relu_done dots_added bias_product bias_row v_turned v_hi_done v_lo_done",
                      "mask_done biasm_done logits_done logits_read shifted exp_done prob_done",
                      "turn_done pt_hi_done pt_lo_done attn_done attn_hi_done attn_lo_done",
                      "s5_scaled s5_exp s5_angles s5_sines s5_tables s5_padded bb_turned bb_kept",
                      "bu_done states_done y_done slots_set gate_done gelu_in gelu_mid gelu_done",
                      "mem_hi_done mem_lo_done mem_summed mem_total conv_in conv_done silu_done h_ready",
                      "gained scaled_v scaled_p newton_done",
                      "y_kept c_set mixed gelu_out glu_done g_hi_done h_hi_done h_lo_done mem_in gate_b_done bu_read"):
            for n in names.split():
                sems[n] = ctx.enter_context(nc.semaphore(n))
        x_in = [ctx.enter_context(nc.semaphore(f"x_in{i}")) for i in range(8)]

        def col(name, i, rows=slice(0, P)):
            return par[rows, bass.ds(i + PCOL[name][0], 1)]

        def whole(name):
            a, n = PCOL[name]
            return par[:, a:a + n]

        ident, causal = whole("ident"), whole("causal")
        block = ctx.enter_context(nc.Block())

        @block.sync
        def _(sp):
            sp.dma_start(par[:], params).then_inc(sems["params_in"], 16)
            w = Tally(sp)
            for s, pieces in enumerate(((2,), (3,), (4, 5), (6, 7))):
                sp.dma_start(raw[:, s, :], wstream[s]).then_inc(sems[f"raw{s}"], 16)
                for i in pieces:
                    sp.dma_start(res[:, 2 * i:2 * i + 2, :], xt[:, 2 * i:2 * i + 2, :]).then_inc(x_in[i], 16)
            w.at["w_lo"] = Count(0)
            with w.loop(N_UNITS // RING - 1, w_lo=RING) as i:
                for s in range(RING):
                    sp.wait_ge(sems["w_lo"], w.next("w_lo"))
                    sp.dma_start(raw[:, s, :], wstream[(i + 1) * RING + s]).then_inc(sems[f"raw{s}"], 16)
            for n, m in enumerate(V_TILES):
                sp.wait_ge(sems["scaled_v"], n + 1)
                sp.dma_start(out[:, m, :], res[:, m, :]).then_inc(sems["out_stored"], 16)
            sp.wait_ge(sems["out_stored"], 16 * KD)

        @block.tensor
        def _(pe):
            w = Tally(pe)
            w.at["proj_read"] = Count(-2)

            def three(out_, hi_w, lo_w, hi_a, lo_a, start, stop):
                nc.tensor.matmul(out_, hi_w, hi_a, start=start, stop=False)
                nc.tensor.matmul(out_, hi_w, lo_a, start=False, stop=False)
                return nc.tensor.matmul(out_, lo_w, hi_a, start=False, stop=stop)

            def unit(out_, hi, lo, q, last, ready=None, squares=False):
                slot = w.now("unit").const % RING
                pe.wait_ge(sems["w_lo"], w.next("w_lo"))
                for kk in range(UT):
                    if ready:
                        pe.wait_ge(sems[ready], w.next(ready))
                    c = slice(kk * P, (kk + 1) * P)
                    ins = three(out_, whi[:, slot, c], wlo[:, slot, c], hi(q * UT + kk), lo(q * UT + kk),
                                (q == 0) and kk == 0, last and kk == UT - 1)
                    if squares:
                        add_square(q * UT + kk)
                ins.then_inc(sems["units_done"], w.add("units_done"))
                w.move("unit")

            def tiles(t):
                return lambda k: t[:, k, :]

            def add_square(m):
                pe.wait_ge(sems["square_done"], m + 1)
                nc.tensor.matmul(turn[0][:, :], ones[:, :], sq[:, m % 2, :], start=m == 0, stop=m == KD - 1).then_inc(
                    sems["square_read"], 1)

            def project(hi, lo, units, cols=T, ready=None, between=(), to=None, squares=False):
                out_ = (to or proj[w.now("block").const % 2])[:, 0:cols]
                if w.due("proj_read"):
                    pe.wait_ge(sems["proj_read"], w.value("proj_read"))
                for q in range(units):
                    unit(out_, tiles(hi), tiles(lo), q, q == units - 1, ready=ready, squares=squares)
                    if q < len(between) and between[q]:
                        between[q]()
                w.move("block")

            def total():
                pe.wait_ge(sems["square_read"], w.next("square_read", KD))
                nc.tensor.matmul(turn[0][:, :], ones[:, :], sumsq[:, :], start=True, stop=True).then_inc(
                    sems["sumsq_total"], w.add("sumsq_total"))

            pe.wait_ge(sems["ones_set"], 1)
            project(act_hi, act_lo, UNITS_D, ready="act_lo_done", squares=True)
            w.at["square_read"] = Count(KD)
            project(act_hi, act_lo, UNITS_D)
            pe.wait_ge(sems["s5_in"], 96)
            nc.tensor.matmul(turn[1][0:HEADS, :], rel_sb[0:BUCKETS, :], onehot_sb[0:BUCKETS, 0:T], start=True, stop=True)
            nc.tensor.matmul(turn[2][0:HEADS, 0:P], rel_sb[0:BUCKETS, :], onehot_sb[0:BUCKETS, T:SPAN],
                             start=True, stop=True).then_inc(sems["bias_product"], w.add("bias_product"))
            pe.wait_ge(sems["proj_read"], 1)
            for t in range(1, QT):
                ins = nc.tensor.transpose(turn[0][:, t * IH:(t + 1) * IH], stage[ID:ID + IH, 0, t * P:(t + 1) * P],
                                          ident[ID:ID + IH, ID:ID + IH])
            ins.then_inc(sems["wi_turned"], w.add("wi_turned"))
            project(act_hi, act_lo, UNITS_D)
            with w.loop(3, w_lo=2 * UNITS_D, units_done=2 * UNITS_D, unit=2 * UNITS_D, block=2, proj_read=2):
                for _ in range(2):
                    project(act_hi, act_lo, UNITS_D)
            pe.wait_ge(sems["s5_padded"], w.next("s5_padded"))
            pe.wait_ge(sems["bias_row"], 1)
            for dst, src in ((turn[1], bb_re), (turn[2], bb_im)):
                for jb in range(SB):
                    ins = nc.tensor.transpose(dst[:, jb * P:(jb + 1) * P], src[:, jb * P:(jb + 1) * P], ident)
                ins.then_inc(sems["bb_turned"], w.add("bb_turned"))

            pe.wait_ge(sems["dup_in"], 32)
            w.at["relu_done"] = Count(-2)
            for t in range(QT - 1, 0, -1):
                for h in range(IH):
                    if t == QT - 1 and h % 2 == 0:
                        pe.wait_ge(sems["lo_done"], h // 2 + 2)
                    if w.due("relu_done"):
                        pe.wait_ge(sems["relu_done"], w.value("relu_done"))
                    r, c = slice(ID * (h % 2), ID * (h % 2 + 1)), slice(t * P, (t + 1) * P)
                    three(pair[h % 2][:, 0:KEYS[t]], qi_hi[r, h // 2, c], qi_lo[r, h // 2, c],
                          ki_hi[r, 0:KEYS[t]], ki_lo[r, 0:KEYS[t]], True, True).then_inc(
                              sems["dots_done"], w.add("dots_done"))

            def turn_v(j):
                pe.wait_ge(sems["proj_read"], w.now("staged").plus(1).value())
                slot = w.now("staged").const % 2
                pe.wait_ge(sems["bb_kept"], 2)
                for kt in range(QT):
                    ins = nc.tensor.transpose(turn[1 + j][:, kt * P:(kt + 1) * P], stage[:, slot, kt * P:(kt + 1) * P], ident)
                ins.then_inc(sems["v_turned"], w.add("v_turned"))

            for _ in range(2):
                project(act_hi, act_lo, UNITS_D)
            project(act_hi, act_lo, UNITS_D)
            w.at["staged"] = w.now("block").plus(-1)
            project(act_hi, act_lo, UNITS_D, between=(None, lambda: turn_v(0)))
            w.at["staged"] = w.now("block").plus(-1)
            project(act_hi, act_lo, UNITS_D, between=(None, lambda: turn_v(1)))
            project(act_hi, act_lo, UNITS_D)

            def logits(h):
                pe.wait_ge(sems["lo_done"], w.next("lo_done:q"))
                for n, t in enumerate(range(QT - 1, -1, -1)):
                    if w.due("logits_read"):
                        pe.wait_ge(sems["logits_read"], w.value("logits_read"))
                    c = slice(t * P, (t + 1) * P)
                    kv = h // (HEADS // KVH)
                    three(pair[n % 2][:, 0:KEYS[t]], q_hi[:, c], q_lo[:, c],
                          k_hi[:, kv, 0:KEYS[t]], k_lo[:, kv, 0:KEYS[t]], True, True).then_inc(
                              sems["logits_done"], w.add("logits_done"))

            def turn_prob():
                pe.wait_ge(sems["prob_done"], w.next("prob_done"))
                if w.due("pt_lo_done:free", 3):
                    pe.wait_ge(sems["pt_lo_done"], w.value("pt_lo_done:free"))
                for b, kts in enumerate(((0,), (1,), (2, 3))):
                    at = 0
                    for kt in kts:
                        for t in range(kt, QT):
                            ins = nc.tensor.transpose(turn[b][:, at:at + P],
                                                      prob[:, OFF[t] + kt * P:OFF[t] + (kt + 1) * P], ident)
                            at += P
                    ins.then_inc(sems["turn_done"], w.add("turn_done"))

            def weigh(h):
                kv = h // (HEADS // KVH)
                pe.wait_ge(sems["pt_lo_done"], w.next("pt_lo_done", 3))
                if w.due("attn_lo_done"):
                    pe.wait_ge(sems["attn_lo_done"], w.value("attn_lo_done"))
                for kt in range(QT):
                    a, n = KOFF[kt], T - kt * P
                    c = slice(kv * P, (kv + 1) * P)
                    ins = three(attn[:, kt * P:T], v_hi[:, kt, c], v_lo[:, kt, c],
                                pt_hi[:, a:a + n], pt_lo[:, a:a + n], kt == 0, kt == QT - 1)
                ins.then_inc(sems["attn_done"], w.add("attn_done"))

            def head(h):
                project(act_hi, act_lo, UNITS_D,
                        between=((lambda: logits(h - 1)) if h >= 1 else None,
                                 (lambda: weigh(h - 2)) if h >= 2 else None, None,
                                 turn_prob if h >= 1 else None))

            w.at.update({"logits_read": Count(-2), "pt_lo_done:free": Count(-3), "attn_lo_done": Count(-1)})
            w.at["lo_done:q"] = Count(N_SPLIT_BEFORE_Q)
            pe.wait_ge(sems["relu_done"], 3 * IH)
            pe.wait_ge(sems["v_lo_done"], 2)
            for h in range(HEADS):
                head(h)
            project(act_hi, act_lo, UNITS_D, between=(lambda: logits(HEADS - 1), lambda: weigh(HEADS - 2), None, turn_prob))
            project(act_hi, act_lo, UNITS_D, between=(None, lambda: weigh(HEADS - 1)))

            def drive(jj):
                if w.due("bu_read"):
                    pe.wait_ge(sems["bu_read"], w.value("bu_read"))
                if jj == 0:
                    pe.wait_ge(sems["slots_set"], w.next("slots_set"))
                r = slice(32 * jj, 32 * (jj + 1))
                nc.tensor.matmul(pair[0][:, :], bb_now[r, 0, :], u_now[r, :], start=True, stop=True)
                nc.tensor.matmul(pair[1][:, :], bb_now[r, 1, :], u_now[r, :], start=True, stop=True).then_inc(
                    sems["bu_done"], w.add("bu_done"))

            def read_out(jj):
                pe.wait_ge(sems["states_done"], w.next("states_done"))
                if jj == 0:
                    pe.wait_ge(sems["c_set"], w.next("c_set"))
                if w.due("y_kept"):
                    pe.wait_ge(sems["y_kept"], w.value("y_kept"))
                nc.tensor.matmul(turn[0][0:32, :], c_now[:, 0, jj, :], wr[:, :], start=True, stop=False)
                nc.tensor.matmul(turn[0][0:32, :], c_now[:, 1, jj, :], wi[:, :], start=False, stop=True).then_inc(
                    sems["y_done"], w.add("y_done"))

            def gated(jj, first=False):
                def s5():
                    if not first:
                        read_out((jj - 1) % TPB)
                    drive(jj)
                project(act_hi, act_lo, UNITS_D, between=(None, s5))
                project(ya_hi, ya_lo, 2)

            pe.wait_ge(sems["attn_lo_done"], HEADS)
            w.at.update(bu_read=Count(-1), y_kept=Count(-1))
            gated(0, True)
            for jj in range(1, TPB):
                gated(jj)
            per = TPB * (UNITS_D + 2)
            with w.loop(SB - 1, w_lo=per, units_done=per, unit=per, block=2 * TPB, proj_read=2 * TPB, bu_read=TPB,
                        slots_set=1, bu_done=TPB, states_done=TPB, y_kept=TPB, c_set=1, y_done=TPB):
                for jj in range(TPB):
                    gated(jj)

            project(act_hi, act_lo, UNITS_D, between=(None, lambda: read_out(TPB - 1)))
            project(act_hi, act_lo, UNITS_D)
            two = dict(w_lo=2 * UNITS_D, units_done=2 * UNITS_D, unit=2 * UNITS_D, block=2, proj_read=2)
            with w.loop(3, **two):
                for _ in range(2):
                    project(act_hi, act_lo, UNITS_D)
            pe.wait_ge(sems["gelu_done"], SB)
            for _ in range(SB):
                project(g_hi, g_lo, 1)
            with w.loop(4, **two):
                for _ in range(2):
                    project(act_hi, act_lo, UNITS_D)
            pe.wait_ge(sems["lo_done"], N_SPLIT_BEFORE_B)
            four = dict(w_lo=4, units_done=4, unit=4, block=4, proj_read=4)
            w.move("proj_read", -2)
            with w.loop(4, **four):
                for k in range(4):
                    project(yb_hi, yb_lo, 1, to=down_bank[k])
            w.move("proj_read", 2)
            project(act_hi, act_lo, UNITS_D, ready="act_lo_done")
            project(act_hi, act_lo, UNITS_D)
            with w.loop(7, **two):
                for _ in range(2):
                    project(act_hi, act_lo, UNITS_D)

            pe.wait_ge(sems["mem_summed"], w.next("mem_summed"))
            nc.tensor.matmul(turn[1][:, 0:M], ones[:, :], mem_acc[:, :], start=True, stop=True)
            for t in range(MT):
                ins = nc.tensor.matmul(turn[1][:, M + t:M + t + 1], mem_acc[:, t * P:(t + 1) * P], ones[:, 0:1],
                                       start=True, stop=True)
            ins.then_inc(sems["mem_total"], w.add("mem_total"))
            pe.wait_ge(sems["mem_lo_done"], KD)
            w.move("proj_read", -2)
            for h in range(XH):
                project(mem_hi, mem_lo, UNITS_D, M, to=down_bank[h])
                if h == 1:
                    total()
            w.move("proj_read", 2)
            pe.wait_ge(sems["proj_read"], w.value("proj_read"))
            for k in range(KD):
                slot = w.now("unit").const % RING
                pe.wait_ge(sems["w_lo"], w.next("w_lo"))
                for t in range(MT):
                    c = slice(t * P, (t + 1) * P)
                    ins = three(pair[t][:, :], mem_hi[:, k, c], mem_lo[:, k, c], whi[:, slot, :], wlo[:, slot, :],
                                k == 0, k == KD - 1)
                ins.then_inc(sems["units_done"], w.add("units_done"))
                w.move("unit")

            def x_logits(h):
                pe.wait_ge(sems["lo_done"], w.next("lo_done:q"))
                if h == 0:
                    pe.wait_ge(sems["logits_read"], HEADS * QT + MT)
                for t in range(QT):
                    if t % 2 == 0:
                        if w.due("exp_done:free", 2):
                            pe.wait_ge(sems["exp_done"], w.value("exp_done:free"))
                    c = slice(t * P, (t + 1) * P)
                    ins = three(pair[t // 2][:, (t % 2) * M:(t % 2 + 1) * M], xq_hi[:, c], xq_lo[:, c],
                                kc_hi[:, h, :], kc_lo[:, h, :], True, True)
                    if t % 2:
                        ins.then_inc(sems["logits_done"], w.add("logits_done"))

            def x_turn():
                pe.wait_ge(sems["prob_done"], w.next("prob_done"))
                if w.due("pt_lo_done:free", MT):
                    pe.wait_ge(sems["pt_lo_done"], w.value("pt_lo_done:free"))
                for b in range(MT):
                    for t in range(QT):
                        ins = nc.tensor.transpose(turn[b][:, t * P:(t + 1) * P], xprob[:, t, b * P:(b + 1) * P], ident)
                    ins.then_inc(sems["turn_done"], w.add("turn_done"))

            def x_weigh(h):
                pe.wait_ge(sems["pt_lo_done"], w.next("pt_lo_done", MT))
                if w.due("attn_lo_done"):
                    pe.wait_ge(sems["attn_lo_done"], w.value("attn_lo_done"))
                for b in range(MT):
                    c = slice(h * P, (h + 1) * P)
                    ins = three(attn[:, :], vc_hi[:, b, c], vc_lo[:, b, c], xpt_hi[:, b, :], xpt_lo[:, b, :],
                                b == 0, b == MT - 1)
                ins.then_inc(sems["attn_done"], w.add("attn_done"))

            w.at["lo_done:q"] = Count(N_SPLIT_BEFORE_XQ)
            w.at["exp_done:free"] = Count(HEADS * QT - QT)
            w.at["pt_lo_done:free"] = Count(HEADS * 3 - MT)
            w.at["act_lo_done"] = Count(2 * KD)
            for h in range(XH):
                project(act_hi, act_lo, UNITS_D, ready="act_lo_done" if h == 0 else None,
                        between=((lambda: x_logits(h - 1)) if h >= 1 else None,
                                 (lambda: x_weigh(h - 2)) if h >= 2 else None, None,
                                 x_turn if h >= 1 else None))
            def out_part(heads, first=False, last=False):
                for m in range(EARLY):
                    slot = (w.now("unit").const + m) % RING
                    if first:
                        pe.wait_ge(sems["w_lo"], w.next("w_lo"))
                    for h in heads:
                        c = slice(h * P, (h + 1) * P)
                        ins = three(out_bank[m][:, :], whi[:, slot, c], wlo[:, slot, c], oc_hi[:, h, :], oc_lo[:, h, :],
                                    first and h == heads[0], last)
                    if last:
                        ins.then_inc(sems["units_done"], w.add("units_done"))

            x_logits(XH - 1)
            x_weigh(XH - 2)
            pe.wait_ge(sems["attn_lo_done"], HEADS + XH - 2)
            out_part(range(XH - 2), first=True)
            x_turn()
            pe.wait_ge(sems["attn_lo_done"], HEADS + XH - 1)
            out_part([XH - 2])
            x_weigh(XH - 1)
            pe.wait_ge(sems["attn_lo_done"], HEADS + XH)
            out_part([XH - 1], last=True)
            w.move("unit", EARLY)
            w.move("block", EARLY)
            w.move("proj_read", EARLY - 2)
            project(oc_hi, oc_lo, 1, to=out_bank[3])
            with w.loop(3, **four):
                for k in range(4):
                    project(oc_hi, oc_lo, 1, to=out_bank[k])
            w.move("proj_read", 2)

            def up():
                for _ in range(2):
                    project(act_hi, act_lo, UNITS_D)

            def down(part, last=False):
                hi, lo = h_hi[:, part * CH:(part + 1) * CH, :], h_lo[:, part * CH:(part + 1) * CH, :]
                w.move("h_lo_done", CH)
                count = w.register("h_lo_done")
                pe.wait_ge(sems["ones_set"], 1)
                pe.wait_ge(sems["h_lo_done"], count)
                w.move("proj_read", -2)
                with w.loop(4, **four):
                    for k in range(4):
                        project(hi, lo, 1, to=down_bank[k])
                w.move("proj_read", 2)

            w.at["act_lo_done"] = Count(3 * KD)
            project(act_hi, act_lo, UNITS_D, ready="act_lo_done", between=(None, total))
            project(act_hi, act_lo, UNITS_D)
            pair_of = {k: 2 * v for k, v in dict(w_lo=UNITS_D, units_done=UNITS_D, unit=UNITS_D, block=1, proj_read=1).items()}
            with w.loop(3, **pair_of):
                up()
            n = 2 * CH * 2 * UNITS_D + 2 * 16
            with w.loop((NCH - 1) // 2, w_lo=n, units_done=n, unit=n, block=2 * (2 * CH + 16), proj_read=2 * (2 * CH + 16),
                        h_lo_done=2 * CH):
                for part in range(2):
                    up()
                    down(part)
                    with w.loop(3, **pair_of):
                        up()
            hi, lo = tiles(h_hi[:, 0:CH, :]), tiles(h_lo[:, 0:CH, :])
            w.move("proj_read", -2)
            pe.wait_ge(sems["h_lo_done"], w.next("h_lo_done", CH - 1))
            for k in range(4):
                pe.wait_ge(sems["w_lo"], w.next("w_lo"))
                pe.wait_ge(sems["proj_read"], w.next("proj_read"))
                for kk in range(CH - 1):
                    c = slice(kk * P, (kk + 1) * P)
                    three(down_bank[k][:, :], whi[:, k, c], wlo[:, k, c], hi(kk), lo(kk), kk == 0, False)
            pe.wait_ge(sems["h_lo_done"], w.next("h_lo_done"))
            for k in range(4):
                c = slice((CH - 1) * P, CH * P)
                three(down_bank[k][:, :], whi[:, k, c], wlo[:, k, c], hi(CH - 1), lo(CH - 1), False, True).then_inc(
                    sems["units_done"], w.add("units_done"))
            w.move("unit", 4)
            w.move("block", 4)
            with w.loop(3, **four):
                for k in range(4):
                    project(h_hi[:, 0:CH, :], h_lo[:, 0:CH, :], 1, to=down_bank[k])
            pe.wait_ge(sems["square_read"], w.next("square_read", KD - LAST_SQUARES))
            nc.tensor.matmul(turn[0][:, :], ones[:, :], sumsq[:, :], start=True, stop=False)
            for m in range(KD - LAST_SQUARES, KD):
                pe.wait_ge(sems["square_done"], 3 * KD + m + 1)
                nc.tensor.matmul(turn[0][:, :], ones[:, :], sq[:, m % 2, :], start=False, stop=m == KD - 1).then_inc(
                    sems["square_read"], w.add("square_read"))

        @block.vector
        def _(dve):
            w = Tally(dve)

            def step(ins):
                ins.then_inc(sems["dve_step"], w.add("dve_step"))
                dve.wait_ge(sems["dve_step"], w.value("dve_step"))

            def mult(out_, a, b):
                return nc.vector.tensor_tensor(out_, a, b, ALU.mult)

            def minus(out_, a, b):
                return nc.vector.tensor_tensor(out_, a, b, ALU.subtract)

            def plus(out_, a, b):
                return nc.vector.tensor_tensor(out_, a, b, ALU.add)

            def cut(k=1):
                for _ in range(k):
                    slot = w.now("cut").const % RING
                    dve.wait_ge(sems["w_hi"], w.next("w_hi"))
                    minus(wlo[:, slot, :], raw[:, slot, :], whi[:, slot, :].bitcast(F32)).then_inc(
                        sems["w_lo"], w.add("w_lo"))
                    w.move("cut")

            def arrived(units):
                dve.wait_ge(sems["units_done"], w.next("units_done", units))
                b = w.now("block").const % 2
                w.move("block")
                return proj[b], b

            def scaled(units, extra=None, cols=slice(0, T), by=None):
                src, b = arrived(units)
                by = rstd[:, :] if by is None else by
                dst = stage[:, b, cols]
                if extra is None:
                    ins = mult(dst, src[:, cols], by)
                else:
                    ins = nc.vector.scalar_tensor_tensor(out=dst, in0=src[:, cols], scalar=extra, in1=by,
                                                         op0=ALU.mult, op1=ALU.mult)
                ins.then_inc(sems["proj_read"], w.add("proj_read"))
                return b

            def low(dst, b, cols=slice(0, T), rows=slice(0, P), hi=None):
                dve.wait_ge(sems["hi_done"], w.next("hi_done"))
                minus(dst, stage[rows, b, cols], hi.bitcast(F32)).then_inc(sems["lo_done"], w.add("lo_done"))

            def inverse_rms(squares=0):
                if squares:
                    dve.wait_ge(sems["square_read"], squares)
                else:
                    dve.wait_ge(sems["sumsq_total"], w.next("sumsq_total"))
                v, t = sq[:, 1, :], sq[:, 0, :]
                step(nc.vector.tensor_scalar(v, turn[0][:, :], 1.0 / D, EPS, ALU.mult, ALU.add))
                nc.vector.reciprocal(rstd[:, :], v).then_inc(sems["inverse_done"], w.add("inverse_done"))
                dve.wait_ge(sems["root_done"], w.next("root_done"))
                newton(rstd[:, :], v, t)

            def newton(y, v, t):
                step(mult(t, y, y))
                step(mult(t, t, v))
                step(nc.vector.tensor_scalar(t, t, -0.5, 1.5, ALU.mult, ALU.add))
                step(mult(y, y, t))

            nc.vector.memset(ones[:, :], 1.0).then_inc(sems["ones_set"], w.add("ones_set"))
            dve.wait_ge(sems["params_in"], 16)
            w.at["cut"] = Count(0)

            def low_tile(i, gain):
                dve.wait_ge(sems["act_hi_done"], w.next("act_hi_done"))
                nc.vector.scalar_tensor_tensor(out=act_lo[:, bass.ds(i, 1), :].squeeze(1), in0=res[:, bass.ds(i, 1), :].squeeze(1),
                                               scalar=col(gain, i), in1=act_hi[:, bass.ds(i, 1), :].squeeze(1).bitcast(F32),
                                               op0=ALU.mult, op1=ALU.subtract).then_inc(
                                                   sems["act_lo_done"], w.add("act_lo_done"))

            cut()
            for k in range(KD):
                low_tile(k, "g_mix")
                if k % UT == UT - 1:
                    cut(FIRST_CUTS[k // UT])
            inverse_rms(squares=KD)
            cut()
            b = scaled(UNITS_D)
            dve.wait_ge(sems["hi_done"], w.next("hi_done"))
            minus(ki_lo[0:ID, :], stage[0:ID, b, :], ki_hi[0:ID, :].bitcast(F32)).then_inc(sems["lo_done"], w.add("lo_done"))
            def indexer_block(i, ahead=True):
                if ahead:
                    cut(UNITS_D)
                b = scaled(UNITS_D)
                dve.wait_ge(sems["hi_done"], w.next("hi_done"))
                minus(qi_lo[:, bass.ds(i, 1), :].squeeze(1), stage[:, b, :],
                      qi_hi[:, bass.ds(i, 1), :].squeeze(1).bitcast(F32)).then_inc(sems["lo_done"], w.add("lo_done"))

            cut(UNITS_D)
            dve.wait_ge(sems["bias_product"], w.next("bias_product"))
            dve.wait_ge(sems["square_done"], KD)
            step(nc.vector.tensor_copy(prob[0:HEADS, 0:T], turn[1][0:HEADS, :]))
            nc.vector.tensor_copy(prob[0:HEADS, T:SPAN], turn[2][0:HEADS, 0:P]).then_inc(sems["bias_row"], w.add("bias_row"))
            dve.wait_ge(sems["wi_turned"], w.next("wi_turned"))
            step(nc.vector.tensor_scalar(widx[:, 1:QT, :], turn[0][:, IH:QT * IH].rearrange("p (t h) -> p t h", t=QT - 1),
                                         WSCALE, None, ALU.mult))
            indexer_block(0, ahead=False)
            def sp(j):
                return s5p[:, j, :]

            lr, li = whole("lam_re"), whole("lam_im")
            dve.wait_ge(sems["s5_exp"], w.next("s5_exp"))
            step(mult(sp(1), lr, sp(0)))
            mult(sp(2), li, sp(0)).then_inc(sems["s5_scaled"], w.add("s5_scaled"))
            dve.wait_ge(sems["s5_scaled"], w.value("s5_scaled"))
            cut()
            step(nc.vector.tensor_scalar(sp(3), sp(2), 1.0 / TWO_PI, ROUND, ALU.mult, ALU.add))
            step(nc.vector.tensor_scalar(sp(3), sp(3), -ROUND, None, ALU.add))
            for part in (C1, C2):
                step(nc.vector.scalar_tensor_tensor(out=sp(2), in0=sp(3), scalar=-part, in1=sp(2), op0=ALU.mult, op1=ALU.add))
            step(nc.vector.tensor_scalar(sp(4), sp(2), TWO_PI / 4, None, ALU.add))
            step(nc.vector.tensor_scalar(sp(7), sp(4), TWO_PI / 2, -TWO_PI, ALU.is_gt, ALU.mult))
            step(plus(sp(4), sp(4), sp(7)))
            step(nc.vector.tensor_scalar(sp(4), sp(4), PI_IN, -PI_IN, ALU.min, ALU.max))
            nc.vector.tensor_scalar(sp(2), sp(2), PI_IN, -PI_IN, ALU.min, ALU.max).then_inc(
                sems["s5_angles"], w.add("s5_angles"))
            cut()
            dve.wait_ge(sems["s5_exp"], w.next("s5_exp"))
            dve.wait_ge(sems["s5_sines"], w.next("s5_sines", 2))
            step(mult(sp(7), mag[:, :], sp(6)))
            step(mult(sp(8), mag[:, :], sp(5)))
            step(nc.vector.tensor_scalar(sp(7), sp(7), -1.0, None, ALU.add))
            step(mult(sp(9), lr, lr))
            step(mult(sp(10), li, li))
            step(plus(sp(9), sp(9), sp(10)))
            step(nc.vector.reciprocal(sp(9), sp(9)))
            cut()
            for dst, (a1, b1, a2, b2, op) in ((11, (7, lr, 8, li, plus)), (12, (8, lr, 7, li, minus))):
                step(mult(sp(dst), sp(a1), b1))
                step(mult(sp(13), sp(a2), b2))
                step(op(sp(dst), sp(dst), sp(13)))
                step(mult(sp(dst), sp(dst), sp(9)))
            cut()
            wide = [P, ST, 2 * GC]
            cr, ci = (sp(j).unsqueeze(2).to_broadcast(wide) for j in (11, 12))
            br, bi, t = (s5t[:, j, :].rearrange("p (j c) -> p j c", c=2 * GC) for j in (0, 1, 2))
            dve.wait_ge(sems["s5_in"], 96)
            for dst, x, y, op in ((bb_re, br, bi, minus), (bb_im, bi, br, plus)):
                d = dst[:, :].rearrange("p (j c) -> p j c", c=2 * GC)
                step(mult(d, x, cr))
                step(mult(t, y, ci))
                ins = op(d, d, t)
                if dst is bb_re:
                    step(ins)
                else:
                    ins.then_inc(sems["s5_padded"], w.add("s5_padded"))
            indexer_block(1, ahead=False)
            with w.loop(3, w_hi=8, w_lo=8, cut=8, units_done=8, block=2, proj_read=2, hi_done=2, lo_done=2) as i:
                indexer_block(i * 2 + 2)
                indexer_block(i * 2 + 3)

            for dst, src in ((bbt_re, turn[1]), (bbt_im, turn[2])):
                dve.wait_ge(sems["bb_turned"], w.next("bb_turned"))
                nc.vector.tensor_copy(dst[:, :, :], src[:, :].rearrange("p (j s) -> p j s", j=SB)).then_inc(
                    sems["bb_kept"], w.add("bb_kept"))

            for t in range(QT - 1, 0, -1):
                s = score[:, OFF[t] - P:OFF[t] - P + KEYS[t]]
                step(nc.vector.memset(s, 0.0))
                with w.loop(IH // 2, relu_done=2, dots_added=2) as i:
                    for hh in range(2):
                        dve.wait_ge(sems["relu_done"], w.next("relu_done"))
                        nc.vector.scalar_tensor_tensor(
                      out=s, in0=relu[:, hh, 0:KEYS[t]], scalar=widx[:, t, bass.ds(i * 2 + hh, 1)], in1=s,
                      op0=ALU.mult, op1=ALU.add).then_inc(sems["dots_added"], w.add("dots_added"))
                        dve.wait_ge(sems["dots_added"], w.value("dots_added"))
                last = s[:, KEYS[t] - P:KEYS[t]]
                step(plus(last, last, causal))

            def rounds(src, last=False):
                def settled():
                    count = w.register("dve_step")
                    dve.wait_ge(sems["ones_set"], 1)
                    dve.wait_ge(sems["dve_step"], count)

                for t in range(QT - 1, 0, -1):
                    a, n = OFF[t] - P, KEYS[t]
                    nc.vector.max(small[:, 16 + 8 * t:24 + 8 * t], src[:, a:a + n]).then_inc(sems["dve_step"], w.add("dve_step"))
                settled()
                if not last:
                    for t in range(QT - 1, 0, -1):
                        a, n = OFF[t] - P, KEYS[t]
                        nc.vector.match_replace(work[:, a:a + n], small[:, 16 + 8 * t:24 + 8 * t], src[:, a:a + n],
                                                LOWEST).then_inc(sems["dve_step"], w.add("dve_step"))
                    settled()

            def more(k):
                with w.loop(k, dve_step=6):
                    rounds(work)

            dve.wait_ge(sems["units_done"], UNITS_D * 9)
            rounds(score)

            def key_block(j):
                b = scaled(UNITS_D)
                dve.wait_ge(sems["hi_done"], w.next("hi_done"))
                minus(k_lo[:, j, :], stage[:, b, :], k_hi[:, j, :].bitcast(F32)).then_inc(sems["lo_done"], w.add("lo_done"))

            def value_low(j):
                dve.wait_ge(sems["v_hi_done"], w.next("v_hi_done"))
                minus(v_lo[:, :, j * P:(j + 1) * P], turn[1 + j][:, :].rearrange("p (t d) -> p t d", t=QT),
                      v_hi[:, :, j * P:(j + 1) * P].bitcast(F32)).then_inc(sems["v_lo_done"], w.add("v_lo_done"))

            def s_block(j):
                src, _ = arrived(UNITS_D)
                mult(s_in[:, j, :], src[:, :], rstd[:, :]).then_inc(sems["proj_read"], w.add("proj_read"))

            assert TOPK // 8 == 16
            more(2)
            key_block(0)
            more(3)
            key_block(1)
            more(2)
            scaled(UNITS_D)
            more(3)
            scaled(UNITS_D)
            value_low(0)
            more(2)
            s_block(2)
            value_low(1)
            more(2)
            rounds(work, last=True)
            s_block(3)

            step(nc.vector.tensor_copy(mask[:, 0:P], causal))
            for t in range(QT - 1, 0, -1):
                n = KEYS[t]
                s, m, e = score[:, OFF[t] - P:OFF[t] - P + n], mask[:, OFF[t]:OFF[t] + n], work2[:, 0:n]
                thr, room = small[:, 16 + 8 * t + 7:16 + 8 * t + 8], small[:, 48 + t:49 + t]
                above = work[:, OFF[t] - P:OFF[t] - P + n]
                step(nc.vector.tensor_scalar(above, s, thr, None, ALU.is_gt, ALU.add, accum_out=room))
                step(nc.vector.tensor_scalar(room, room, -1.0, float(TOPK), ALU.mult, ALU.add))
                step(nc.vector.tensor_scalar(e, s, thr, None, ALU.is_equal))
                step(nc.vector.tensor_tensor_scan(m, ones[:, 0:1].to_broadcast([P, n]), e, 0.0, ALU.mult, ALU.add))
                step(nc.vector.scalar_tensor_tensor(out=m, in0=m, scalar=room, in1=e, op0=ALU.is_le, op1=ALU.mult))
                step(plus(m, m, above))
                ins = nc.vector.tensor_scalar(m, m, -NEG, NEG, ALU.mult, ALU.add)
                if t == 1:
                    ins.then_inc(sems["mask_done"], w.add("mask_done"))
                    dve.wait_ge(sems["mask_done"], w.value("mask_done"))
                else:
                    step(ins)

            def softmax_in():
                dve.wait_ge(sems["biasm_done"], w.next("biasm_done"))
                for n, t in enumerate(range(QT - 1, -1, -1)):
                    dve.wait_ge(sems["logits_done"], w.next("logits_done"))
                    a, k = OFF[t], KEYS[t]
                    nc.vector.tensor_tensor_reduce(
                  out=prob[:, a:a + k], in0=pair[n % 2][:, 0:k], in1=biasm[:, a:a + k], scale=1.0, scalar=LOWEST,
                  op0=ALU.add, op1=ALU.max, accum_out=small[:, t:t + 1]).then_inc(sems["logits_read"], w.add("logits_read"))
                dve.wait_ge(sems["logits_read"], w.value("logits_read"))
                nc.vector.tensor_scalar(small[:, 4:8], small[:, 0:4], -1.0, None, ALU.mult).then_inc(
                    sems["shifted"], w.add("shifted"))

            def softmax_out(parts):
                dve.wait_ge(sems["exp_done"], w.next("exp_done", QT))
                step(nc.vector.reciprocal(small[:, 12:16], small[:, 8:12]))
                for t, part in enumerate(parts):
                    ins = nc.vector.tensor_scalar(part, part, small[:, 12 + t:13 + t], None, ALU.mult)
                    if t < QT - 1:
                        ins.then_inc(sems["dve_step"], w.add("dve_step"))
                dve.wait_ge(sems["dve_step"], w.value("dve_step"))
                ins.then_inc(sems["prob_done"], w.add("prob_done"))

            def turned_low(parts):
                for b, (dst, hi, n) in enumerate(parts):
                    dve.wait_ge(sems["pt_hi_done"], w.next("pt_hi_done"))
                    minus(dst, turn[b][:, 0:n], hi.bitcast(F32)).then_inc(sems["pt_lo_done"], w.add("pt_lo_done"))

            def attn_low(dst, hi):
                dve.wait_ge(sems["attn_hi_done"], w.next("attn_hi_done"))
                minus(dst, attn[:, :], hi.bitcast(F32)).then_inc(sems["attn_lo_done"], w.add("attn_lo_done"))

            PROBS = [prob[:, OFF[t]:OFF[t] + KEYS[t]] for t in range(QT)]
            TURNED = [(pt_lo[:, a:b], pt_hi[:, a:b], b - a) for a, b in ((0, T), (T, KOFF[2]), (KOFF[2], PAIRS))]

            def query_block(lo, hi, units=UNITS_D):
                b = scaled(units, extra=QS)
                low(lo, b, hi=hi)

            for i in range(HEADS + 2):
                if 1 <= i <= HEADS:
                    softmax_in()
                    softmax_out(PROBS)
                if i >= 2:
                    attn_low(ya_lo[:, i - 2, :], ya_hi[:, i - 2, :])
                if i < HEADS:
                    query_block(q_lo[:, :], q_hi[:, :])
                else:
                    s_block(i - HEADS)
                if 1 <= i <= HEADS:
                    turned_low(TURNED)

            def angles(tile):
                shape = [P, FHI, FLO]

                def long(x):
                    return x[:, :].rearrange("p (a b) -> p a b", b=FLO)

                def fine(x):
                    return x[:, bass.ds(tile, 1), :].to_broadcast(shape)

                def coarse(x):
                    return x[:, bass.ds(tile, 1), :].rearrange("p o a -> p a o").to_broadcast(shape)

                a, b = long(cost), long(sint)
                step(mult(a, coarse(hop_c), fine(tab_c)))
                step(mult(long(rot), coarse(hop_s), fine(tab_s)))
                step(minus(a, a, long(rot)))
                step(mult(b, coarse(hop_s), fine(tab_c)))
                step(mult(long(rot), coarse(hop_c), fine(tab_s)))
                step(plus(b, b, long(rot)))

            def turn_in():
                dve.wait_ge(sems["bu_done"], w.next("bu_done"))
                re, im = pair[0][:, :], pair[1][:, :]
                step(mult(wr[:, :], cost[:, :], re))
                step(mult(rot[:, :], sint[:, :], im))
                step(plus(wr[:, :], wr[:, :], rot[:, :]))
                step(mult(wi[:, :], cost[:, :], im))
                mult(rot[:, :], sint[:, :], re).then_inc(sems["bu_read"], w.add("bu_read"))
                dve.wait_ge(sems["bu_read"], w.value("bu_read"))
                step(minus(wi[:, :], wi[:, :], rot[:, :]))

            def recur(tile):
                m = mag[:, bass.ds(tile, 1)].to_broadcast([P, T])
                step(nc.vector.tensor_tensor_scan(zr[:, :], m, wr[:, :], 0.0, ALU.mult, ALU.add))
                step(nc.vector.tensor_tensor_scan(zi[:, :], m, wi[:, :], 0.0, ALU.mult, ALU.add))

            def turn_back():
                step(mult(wr[:, :], cost[:, :], zr[:, :]))
                step(mult(rot[:, :], sint[:, :], zi[:, :]))
                step(minus(wr[:, :], wr[:, :], rot[:, :]))
                step(mult(wi[:, :], sint[:, :], zr[:, :]))
                step(mult(rot[:, :], cost[:, :], zi[:, :]))
                nc.vector.scalar_tensor_tensor(out=wi[:, :], in0=wi[:, :], scalar=-1.0, in1=rot[:, :],
                                               op0=ALU.mult, op1=ALU.subtract).then_inc(
                                                   sems["states_done"], w.add("states_done"))
                dve.wait_ge(sems["states_done"], w.value("states_done"))

            def keep_y(jb, jj):
                dve.wait_ge(sems["y_done"], w.next("y_done"))
                r = slice(32 * jj, 32 * (jj + 1))
                s = s_in[r, bass.ds(jb, 1), :].squeeze(1)
                nc.vector.scalar_tensor_tensor(out=s, in0=s, scalar=col("d_skip", jb, r), in1=turn[0][0:32, :],
                                               op0=ALU.mult, op1=ALU.add).then_inc(sems["y_kept"], w.add("y_kept"))

            def gated(jb, jj, prev=None):
                tile = jb * TPB + jj
                angles(tile)
                if prev is not None:
                    keep_y(*prev)
                turn_in()
                b = scaled(UNITS_D)
                recur(tile)
                turn_back()
                src, _ = arrived(2)
                dve.wait_ge(sems["gate_done"], w.next("gate_done"))
                mult(res[:, bass.ds(tile, 1), :].squeeze(1), src[:, :], stage[:, b, :]).then_inc(
                    sems["proj_read"], w.add("proj_read"))

            w.at["y_done"] = Count(0)
            gated(0, 0)
            for jj in range(1, TPB):
                gated(0, jj, (0, jj - 1))
            steps = TPB * (6 + 5 + 2 + 5)
            with w.loop(SB - 1, units_done=TPB * (UNITS_D + 2), block=2 * TPB, proj_read=2 * TPB, gate_done=TPB, bu_done=TPB,
                        bu_read=TPB, states_done=TPB, y_done=TPB, y_kept=TPB, dve_step=steps) as i:
                gated(i + 1, 0, (i, TPB - 1))
                for jj in range(1, TPB):
                    gated(i + 1, jj, (i + 1, jj - 1))
            keep_y(SB - 1, TPB - 1)
            dve.wait_ge(sems["y_kept"], w.value("y_kept"))

            def gate_block():
                if w.due("gate_b_done:free"):
                    dve.wait_ge(sems["gate_b_done"], w.value("gate_b_done:free"))
                scaled(UNITS_D)

            w.at["gate_b_done:free"] = Count(-2)

            gate_block()
            for j in range(SB):
                y, t = s_in[:, j, :], zr[:, :]
                if j:
                    dve.wait_ge(sems["gelu_mid"], j)
                step(mult(t, y, y))
                step(nc.vector.tensor_scalar(t, t, 0.044715, 1.0, ALU.mult, ALU.add))
                mult(t, t, y).then_inc(sems["gelu_in"], w.add("gelu_in"))
                dve.wait_ge(sems["gelu_mid"], w.next("gelu_mid"))
                dve.wait_ge(sems["gelu_in"], w.value("gelu_in"))
                mult(y, y, wr[:, :]).then_inc(sems["gelu_out"], w.add("gelu_out"))
                dve.wait_ge(sems["gelu_out"], w.value("gelu_out"))
                if j % 2:
                    gate_block()
            for j in range(SB):
                dve.wait_ge(sems["g_hi_done"], w.next("g_hi_done"))
                minus(g_lo[:, j, :], s_in[:, j, :], g_hi[:, j, :].bitcast(F32)).then_inc(
                    sems["gelu_done"], w.add("gelu_done"))
            for _ in range(5):
                gate_block()
            dve.wait_ge(sems["gate_b_done"], 8)
            for j in range(SB):
                src, b = arrived(1)
                nc.vector.tensor_scalar(stage[:, b, :], src[:, :], col("b_glu", j), None, ALU.add).then_inc(
                    sems["proj_read"], w.add("proj_read"))
                dve.wait_ge(sems["gate_done"], w.next("gate_done"))
                mult(stage[:, b, :], stage[:, b, :], s_in[:, j, :]).then_inc(sems["glu_done"], w.add("glu_done"))
                dve.wait_ge(sems["glu_done"], w.value("glu_done"))
                low(yb_lo[:, j, :], b, hi=yb_hi[:, j, :])
            dve.wait_ge(sems["lo_done"], w.value("lo_done"))
            with w.loop(4, units_done=8, block=2, proj_read=2, **{"gate_b_done:free": 2}):
                gate_block()
                gate_block()

            dve.wait_ge(sems["gate_b_done"], KD)
            def mix_block(m, k):
                _, b = arrived(1)
                r = res[:, bass.ds(m, 1), :].squeeze(1)
                mult(stage[:, b, :], down_bank[k][:, :], sig_b[:, bass.ds(m, 1), :].squeeze(1)).then_inc(
                    sems["proj_read"], w.add("proj_read"))
                dve.wait_ge(sems["proj_read"], w.value("proj_read"))
                plus(r, r, stage[:, b, :]).then_inc(sems["mixed"], w.add("mixed"))

            def mix_low(m):
                dve.wait_ge(sems["act_hi_done"], w.next("act_hi_done"))
                minus(act_lo[:, bass.ds(m, 1), :].squeeze(1), res[:, bass.ds(m, 1), :].squeeze(1),
                      act_hi[:, bass.ds(m, 1), :].squeeze(1).bitcast(F32)).then_inc(
                          sems["act_lo_done"], w.add("act_lo_done"))

            mix_block(0, 0)
            with w.loop(3, units_done=4, block=4, proj_read=4, mixed=4, act_hi_done=4, act_lo_done=4) as i:
                for k in range(1, 5):
                    mix_block(i * 4 + k, k % 4)
                    mix_low(i * 4 + (k - 1))
            for m in range(13, KD):
                mix_block(m, m % 4)
                mix_low(m - 1)
            mix_low(KD - 1)

            def add_block(m, units, at=None):
                src, _ = arrived(units)
                src = at or src
                r = res[:, bass.ds(m, 1), :].squeeze(1)
                plus(r, r, src[:, :]).then_inc(sems["proj_read"], w.add("proj_read"))

            step(nc.vector.memset(mem_acc[:, :], 0.0))

            def mem_low(m):
                r = mem_raw[:, bass.ds(m, 1), :].squeeze(1)
                dve.wait_ge(sems["mem_hi_done"], w.next("mem_hi_done"))
                nc.vector.scalar_tensor_tensor(
                    out=mem_lo[:, bass.ds(m, 1), :].squeeze(1), in0=r, scalar=col("g_mem", m),
                    in1=mem_hi[:, bass.ds(m, 1), :].squeeze(1).bitcast(F32), op0=ALU.mult, op1=ALU.subtract).then_inc(
                        sems["mem_lo_done"], w.add("mem_lo_done"))
                dve.wait_ge(sems["mem_lo_done"], w.value("mem_lo_done"))
                step(mult(r, r, r))
                step(plus(mem_acc[:, :], mem_acc[:, :], r))

            dve.wait_ge(x_in[0], 32)
            add_block(0, UNITS_D)
            add_block(1, UNITS_D)
            for k in range(1, 8):
                dve.wait_ge(x_in[k], 32)
            with w.loop(KD // 2 - 2, units_done=8, block=2, proj_read=2, mem_hi_done=2, mem_lo_done=2, dve_step=4) as i:
                for k in range(2):
                    mem_low(i * 2 + k)
                    add_block(i * 2 + (k + 2), UNITS_D)
            for m in (KD - 2, KD - 1):
                mem_low(2 * m - KD)
                mem_low(2 * m - KD + 1)
                if m == KD - 1:
                    nc.vector.tensor_copy(small[:, 60:61], mem_acc[:, 0:1]).then_inc(sems["mem_summed"], w.add("mem_summed"))
                    dve.wait_ge(sems["mem_summed"], w.value("mem_summed"))
                add_block(m, UNITS_D)
            dve.wait_ge(sems["proj_read"], w.value("proj_read"))

            dve.wait_ge(sems["mem_total"], w.next("mem_total"))
            step(nc.vector.tensor_scalar(vmem[:, :], turn[1][:, 0:M + MT], 1.0 / D, EPS, ALU.mult, ALU.add))
            nc.vector.reciprocal(rmem[:, :], vmem[:, :]).then_inc(sems["inverse_done"], w.add("inverse_done"))
            dve.wait_ge(sems["root_done"], w.next("root_done"))
            newton(rmem[:, :], vmem[:, :], mem_raw[:, 0:2, :].rearrange("p k m -> p (k m)")[:, 0:M + MT])
            MEMC = slice(0, M)

            def mem_key(h):
                _, b = arrived(UNITS_D)
                mult(stage[:, b, MEMC], down_bank[h][:, MEMC], rmem[:, MEMC]).then_inc(sems["proj_read"], w.add("proj_read"))
                low(kc_lo[:, h, :], b, cols=MEMC, hi=kc_hi[:, h, :])

            mem_key(0)
            mem_key(1)
            for k in range(4):
                low_tile(k, "g_cross")
            mem_key(2)
            mem_key(3)
            for k in range(4, 8):
                low_tile(k, "g_cross")
            dve.wait_ge(sems["square_read"], 2 * KD)
            inverse_rms()
            for k in range(8, KD):
                low_tile(k, "g_cross")
            w.at["cut"] = w.at["w_hi"] = w.at["w_lo"] = Count(LAST_POOL_CUT)
            dve.wait_ge(sems["w_lo"], w.value("w_lo"))
            cut(8)
            dve.wait_ge(sems["units_done"], w.next("units_done", KD))
            for t in range(MT):
                nc.vector.tensor_scalar(stage[:, t, :], pair[t][:, :], rmem[:, M + t:M + t + 1], None, ALU.mult).then_inc(
                    sems["logits_read"], w.add("logits_read"))
                dve.wait_ge(sems["v_hi_done"], w.next("v_hi_done"))
                minus(vc_lo[:, t, :], stage[:, t, :], vc_hi[:, t, :].bitcast(F32)).then_inc(
                    sems["v_lo_done"], w.add("v_lo_done"))
            dve.wait_ge(sems["v_lo_done"], w.value("v_lo_done"))
            XPARTS = [xprob[:, t, :] for t in range(QT)]
            XTURNED = [(xpt_lo[:, b, :], xpt_hi[:, b, :], T) for b in range(MT)]
            for i in range(XH + 2):
                if i < XH:
                    cut()
                if 1 <= i <= XH:
                    for half in range(2):
                        dve.wait_ge(sems["logits_done"], w.next("logits_done"))
                        nc.vector.reduce_max(small[:, 2 * half:2 * half + 2],
                                             pair[half][:, :].rearrange("p (t m) -> p t m", t=2), AX_X).then_inc(
                                                 sems["dve_step"], w.add("dve_step"))
                    dve.wait_ge(sems["dve_step"], w.value("dve_step"))
                    nc.vector.tensor_scalar(small[:, 4:8], small[:, 0:4], -1.0, None, ALU.mult).then_inc(
                        sems["shifted"], w.add("shifted"))
                    if i < XH:
                        cut()
                    softmax_out(XPARTS)
                elif i < XH:
                    cut()
                if i >= 2:
                    attn_low(oc_lo[:, i - 2, :], oc_hi[:, i - 2, :])
                if i < XH:
                    cut(2)
                    query_block(xq_lo[:, :], xq_hi[:, :])
                if 1 <= i <= XH:
                    turned_low(XTURNED)
            def out_block(m, k):
                add_block(m, 1, out_bank[k])
                dve.wait_ge(sems["proj_read"], w.value("proj_read"))

            out_block(0, 0)
            cut()
            with w.loop(3, w_hi=4, w_lo=4, cut=4, units_done=4, block=4, proj_read=4, act_hi_done=4, act_lo_done=4) as i:
                for k in range(1, 5):
                    out_block(i * 4 + k, k % 4)
                    low_tile(i * 4 + (k - 1), "g_ffn")
                    cut()
            for m in range(13, KD):
                out_block(m, m % 4)
                low_tile(m - 1, "g_ffn")
                cut()
            low_tile(KD - 1, "g_ffn")

            step(nc.vector.memset(padded[:, :, 0:2], 0.0))

            def up_block(p, which):
                src, b = arrived(UNITS_D)
                blk = p + FB * which
                mult(padded[:, which, 2:T + 2], src[:, :], rstd[:, :]).then_inc(sems["proj_read"], w.add("proj_read"))
                dve.wait_ge(sems["conv_in"], w.next("conv_in"))
                c = conv[:, which, :]
                step(nc.vector.scalar_tensor_tensor(out=c, in0=padded[:, which, 1:T + 1], scalar=col("conv_w", blk * 3 + 1), in1=c,
                                                    op0=ALU.mult, op1=ALU.add))
                nc.vector.scalar_tensor_tensor(out=c, in0=padded[:, which, 0:T], scalar=col("conv_w", blk * 3), in1=c,
                                               op0=ALU.mult, op1=ALU.add).then_inc(sems["conv_done"], w.add("conv_done"))

            def up(p, h_slot, before=None):
                cut(4)
                early = 0
                if before:
                    before()
                    early = 3
                cut(early)
                up_block(p, 0)
                cut(4 - early)
                up_block(p, 1)
                dve.wait_ge(sems["conv_done"], w.value("conv_done"))
                dve.wait_ge(sems["silu_done"], w.next("silu_done"))
                mult(conv[:, 0, :], sigm[:, :], conv[:, 1, :]).then_inc(sems["h_ready"], w.add("h_ready"))
                dve.wait_ge(sems["h_hi_done"], w.next("h_hi_done"))
                minus(h_lo[:, bass.ds(h_slot, 1), :].squeeze(1), conv[:, 0, :],
                      h_hi[:, bass.ds(h_slot, 1), :].squeeze(1).bitcast(F32)).then_inc(sems["h_lo_done"], w.add("h_lo_done"))

            PAIR = dict(w_hi=8, w_lo=8, cut=8, units_done=8, block=2, proj_read=2, conv_in=2, dve_step=2, conv_done=2,
                        silu_done=1, h_ready=1, h_hi_done=1, h_lo_done=1)
            up(0, 0, inverse_rms)
            with w.loop(CH - 1, **PAIR) as i:
                up(i + 1, i + 1)
            n = 16 * CH + 2 * 16
            with w.loop((NCH - 1) // 2, w_hi=n, w_lo=n, cut=n, units_done=n, block=4 * CH + 32, proj_read=4 * CH + 32,
                        conv_in=4 * CH, dve_step=4 * CH, conv_done=4 * CH, silu_done=2 * CH, h_ready=2 * CH,
                        h_hi_done=2 * CH, h_lo_done=2 * CH) as c:
                for part in range(2):
                    first = c * (2 * CH) + CH * (part + 1)
                    h0 = CH * (1 - part)
                    up(first, h0)
                    with w.loop(4, w_hi=4, w_lo=4, cut=4, units_done=4, block=4, proj_read=4) as i:
                        for k in range(4):
                            cut()
                            add_block(i * 4 + k, 1, down_bank[k])
                    with w.loop(CH - 1, **PAIR) as i:
                        up(first + i + 1, i + (h0 + 1))
            with w.loop(3, w_hi=4, w_lo=4, cut=4, units_done=4, block=4, proj_read=4) as i:
                for k in range(4):
                    cut()
                    add_block(i * 4 + k, 1, down_bank[k])
            for k in range(12, KD):
                add_block(k, 1, down_bank[k % 4])

            inverse_rms(squares=4 * KD)
            nc.vector.memset(small[:, 0:1], 0.0).then_inc(sems["newton_done"], w.add("newton_done"))
            for m in V_TILES:
                nc.vector.scalar_tensor_tensor(out=res[:, m, :], in0=res[:, m, :], scalar=col("g_final", m),
                                               in1=rstd[:, :], op0=ALU.mult, op1=ALU.mult).then_inc(
                                                   sems["scaled_v"], w.add("scaled_v"))

        @block.scalar
        def _(act):
            w = Tally(act)
            w.at["square_read:free"] = Count(-2)

            def copy(out_, in_, scale=1.0):
                return nc.scalar.activation(out_, in_, ACT.Copy, scale=scale)

            def at(t, i):
                return t[:, bass.ds(i, 1), :].squeeze(1)

            def cut(k=1):
                for _ in range(k):
                    n = w.now("cut")
                    slot = n.const % RING
                    act.wait_ge(sems[f"raw{slot}"], n.times(16 // RING).plus(16 - 16 // RING * slot).value())
                    if n.const >= RING:
                        act.wait_ge(sems["units_done"], n.plus(1 - RING).value())
                    copy(whi[:, slot, :], raw[:, slot, :]).then_inc(sems["w_hi"], w.add("w_hi"))
                    w.move("cut")

            def high_tile(i, gain):
                act.wait_ge(sems["ones_set"], 1)
                nc.scalar.activation(at(act_hi, i), at(res, i), ACT.Copy, scale=col(gain, i)).then_inc(
                    sems["act_hi_done"], w.add("act_hi_done"))

            def square(i, k):
                if w.due("square_read:free"):
                    count = w.register("square_read:free")
                    act.wait_ge(sems["ones_set"], 1)
                    act.wait_ge(sems["square_read"], count)
                nc.scalar.activation(sq[:, k % 2, :], at(res, i), ACT.Square).then_inc(
                    sems["square_done"], w.add("square_done"))

            def root(x):
                act.wait_ge(sems["inverse_done"], w.next("inverse_done"))
                nc.scalar.activation(x, x, ACT.Sqrt).then_inc(sems["root_done"], w.add("root_done"))

            def staged():
                act.wait_ge(sems["proj_read"], w.next("proj_read"))
                b = w.now("block").const % 2
                w.move("block")
                return b

            def skip(k=1):
                w.move("proj_read", k)
                w.move("block", k)

            def high(dst, cols=slice(0, T), rows=slice(0, P)):
                b = staged()
                act.wait_ge(sems["ones_set"], 1)
                copy(dst, stage[rows, b, cols]).then_inc(sems["hi_done"], w.add("hi_done"))

            for i in (0, 1):
                act.dma_start(res[:, 2 * i:2 * i + 2, :], xt[:, 2 * i:2 * i + 2, :]).then_inc(x_in[i], 16)
            act.wait_ge(sems["params_in"], 16)
            act.wait_ge(sems["ones_set"], 1)
            cut()
            for k in range(KD):
                if k % 2 == 0:
                    act.wait_ge(x_in[k // 2], 16)
                high_tile(k, "g_mix")
                square(k, k)
                if k % UT == UT - 1:
                    cut(FIRST_CUTS[k // UT])
            root(rstd[:, :])
            cut()
            high(ki_hi[0:ID, :], rows=slice(0, ID))

            def indexer_block(i):
                high(at(qi_hi, i))

            cut(4)
            act.wait_ge(sems["bias_row"], w.next("bias_row"))
            act.dma_start(strips[:, :, 0:SPAN], prob[0:HEADS, 0:SPAN].unsqueeze(1).to_broadcast([HEADS, P, SPAN])).then_inc(
                sems["strip_out"], 16)
            act.wait_ge(sems["lo_done"], 1)
            act.dma_start(ki_hi[ID:P, :].bitcast(F32), ki_hi[0:ID, :].bitcast(F32)).then_inc(sems["dup_in"], 16)
            act.dma_start(ki_lo[ID:P, :].bitcast(F32), ki_lo[0:ID, :].bitcast(F32)).then_inc(sems["dup_in"], 16)
            indexer_block(0)
            nc.scalar.activation(s5p[:, 0, :], whole("log_dt"), ACT.Exp).then_inc(sems["s5_exp"], w.add("s5_exp"))
            cut()
            act.wait_ge(sems["s5_scaled"], w.next("s5_scaled"))
            nc.scalar.activation(mag[:, :], s5p[:, 1, :], ACT.Exp).then_inc(sems["s5_exp"], w.add("s5_exp"))
            cut()
            act.wait_ge(sems["s5_angles"], w.next("s5_angles"))
            nc.scalar.activation(s5p[:, 5, :], s5p[:, 2, :], ACT.Sin).then_inc(sems["s5_sines"], w.add("s5_sines"))
            nc.scalar.activation(s5p[:, 6, :], s5p[:, 4, :], ACT.Sin).then_inc(sems["s5_sines"], w.add("s5_sines"))
            cut(2)
            indexer_block(1)
            with w.loop(3, w_hi=8, cut=8, proj_read=2, block=2, hi_done=2) as i:
                for k in range(2):
                    cut(4)
                    indexer_block(i * 2 + (2 + k))

            act.wait_ge(sems["strip_out"], 16)
            w.at["dots_added:free"] = Count(-2)

            def rectify(t, h):
                act.wait_ge(sems["dots_done"], w.next("dots_done"))
                if w.due("dots_added:free"):
                    act.wait_ge(sems["dots_added"], w.value("dots_added:free"))
                nc.scalar.activation(relu[:, h % 2, 0:KEYS[t]], pair[h % 2][:, 0:KEYS[t]], ACT.Relu).then_inc(
                    sems["relu_done"], w.add("relu_done"))

            rectify(QT - 1, 0)
            rectify(QT - 1, 1)
            for t in range(QT - 1, 0, -1):
                with w.loop(IH // 2 - (t == QT - 1), dots_done=2, relu_done=2, **{"dots_added:free": 2}):
                    rectify(t, 0)
                    rectify(t, 1)

            def value_high(j):
                act.wait_ge(sems["v_turned"], w.next("v_turned"))
                copy(v_hi[:, :, j * P:(j + 1) * P], turn[1 + j][:, :].rearrange("p (t d) -> p t d", t=QT)).then_inc(
                    sems["v_hi_done"], w.add("v_hi_done"))

            for j in range(KVH):
                cut(4)
                high(k_hi[:, j, :])
            cut(4)
            skip()
            for j in range(KVH):
                cut(2)
                value_high(j)
                cut(2)
                skip()
            cut(4)
            skip()

            def exps(parts, ins_):
                act.wait_ge(sems["shifted"], w.next("shifted"))
                for t in range(QT):
                    nc.scalar.activation(parts[t], ins_[t], ACT.Exp, bias=small[:, 4 + t:5 + t],
                                         accum_out=small[:, 8 + t:9 + t]).then_inc(sems["exp_done"], w.add("exp_done"))

            def attn_high(dst):
                act.wait_ge(sems["attn_done"], w.next("attn_done"))
                copy(dst, attn[:, :]).then_inc(sems["attn_hi_done"], w.add("attn_hi_done"))

            def turned_high(parts):
                for b, (dst, n) in enumerate(parts):
                    act.wait_ge(sems["turn_done"], w.next("turn_done"))
                    copy(dst, turn[b][:, 0:n]).then_inc(sems["pt_hi_done"], w.add("pt_hi_done"))

            PROBS = [prob[:, OFF[t]:OFF[t] + KEYS[t]] for t in range(QT)]
            TURNED = [(pt_hi[:, a:b], b - a) for a, b in ((0, T), (T, KOFF[2]), (KOFF[2], PAIRS))]
            for i in range(HEADS + 2):
                cut()
                if 1 <= i <= HEADS:
                    exps(PROBS, PROBS)
                cut()
                if i >= 2:
                    attn_high(ya_hi[:, i - 2, :])
                cut(2)
                if i < HEADS:
                    high(q_hi[:, :])
                else:
                    skip()
                if 1 <= i <= HEADS:
                    turned_high(TURNED)

            def gated(jb, jj, tiles_before):
                cut()
                if jj == 0:
                    if tiles_before.const:
                        act.wait_ge(sems["bu_done"], tiles_before.value())
                    act.wait_ge(sems["ones_set"], 1)
                    copy(u_now[:, :], at(s_in, jb))
                    copy(bb_now[:, 0, :], at(bbt_re, jb))
                    copy(bb_now[:, 1, :], at(bbt_im, jb)).then_inc(sems["slots_set"], w.add("slots_set"))
                cut()
                if jj == 0:
                    if tiles_before.const:
                        act.wait_ge(sems["y_done"], tiles_before.value())
                    act.wait_ge(sems["ones_set"], 1)
                    copy(c_now[:, 0, :, :], cc_re[:, bass.ds(jb * TPB, TPB), :])
                    copy(c_now[:, 1, :, :], cc_im[:, bass.ds(jb * TPB, TPB), :]).then_inc(sems["c_set"], w.add("c_set"))
                cut(2)
                b = staged()
                nc.scalar.activation(stage[:, b, :], stage[:, b, :], ACT.Sigmoid).then_inc(
                    sems["gate_done"], w.add("gate_done"))
                cut(2)
                skip()

            act.wait_ge(sems["proj_read"], w.value("proj_read"))
            act.wait_ge(sems["bb_kept"], 2)
            for jj in range(TPB):
                gated(0, jj, Count(0))
            per = TPB * (UNITS_D + 2)
            with w.loop(SB - 1, w_hi=per, cut=per, slots_set=1, c_set=1, proj_read=2 * TPB, block=2 * TPB, gate_done=TPB) as i:
                for jj in range(TPB):
                    gated(i + 1, jj, Count(TPB, ((i, TPB),)))

            def gate_b(m):
                cut(4)
                b = staged()
                act.wait_ge(sems["ones_set"], 1)
                nc.scalar.activation(at(sig_b, m), stage[:, b, :], ACT.Sigmoid).then_inc(
                    sems["gate_b_done"], w.add("gate_b_done"))

            gate_b(0)
            for j in range(SB):
                act.wait_ge(sems["gelu_in"], w.next("gelu_in"))
                nc.scalar.activation(wr[:, :], zr[:, :], ACT.Sigmoid, scale=GELU_C).then_inc(
                    sems["gelu_mid"], w.add("gelu_mid"))
                if j % 2:
                    gate_b(1 + j // 2)
            act.wait_ge(sems["gelu_out"], SB)
            for j in range(SB):
                copy(g_hi[:, j, :], s_in[:, j, :]).then_inc(sems["g_hi_done"], w.add("g_hi_done"))
            for m in range(3, 8):
                gate_b(m)
            for j in range(SB):
                cut()
                b = staged()
                nc.scalar.activation(stage[:, b, :], stage[:, b, :], ACT.Sigmoid).then_inc(
                    sems["gate_done"], w.add("gate_done"))
                act.wait_ge(sems["glu_done"], w.next("glu_done"))
                copy(yb_hi[:, j, :], stage[:, b, :]).then_inc(sems["hi_done"], w.add("hi_done"))
            with w.loop(4, w_hi=8, cut=8, proj_read=2, block=2, gate_b_done=2) as i:
                gate_b(i * 2 + 8)
                gate_b(i * 2 + 9)

            with w.loop(4, w_hi=4, cut=4, mixed=4, act_hi_done=4) as i:
                for k in range(4):
                    cut()
                    act.wait_ge(sems["mixed"], w.next("mixed"))
                    act.wait_ge(sems["ones_set"], 1)
                    copy(at(act_hi, i * 4 + k), at(res, i * 4 + k)).then_inc(sems["act_hi_done"], w.add("act_hi_done"))
            skip(16)
            def fetch_x(i):
                act.wait_ge(sems["act_lo_done"], KD + 2 * (i + 1))
                act.dma_start(res[:, 2 * i:2 * i + 2, :], xt[:, 2 * i:2 * i + 2, :]).then_inc(x_in[i], 16)

            def fetch_mem(i):
                act.wait_ge(sems["act_lo_done"], 2 * KD)
                act.dma_start(mem_raw[:, 4 * i:4 * i + 4, :], memt[:, 4 * i:4 * i + 4, :]).then_inc(sems["mem_in"], 16)

            def mem_high(m):
                act.wait_ge(sems["ones_set"], 1)
                nc.scalar.activation(at(mem_hi, m), at(mem_raw, m), ACT.Copy, scale=col("g_mem", m)).then_inc(
                    sems["mem_hi_done"], w.add("mem_hi_done"))

            def added(m, k):
                staged()
                square(m, k)

            fetch_x(0)
            for i in range(1, 5):
                cut()
                fetch_x(i)
            added(0, 0)
            for i in range(5, 8):
                cut()
                fetch_x(i)
            cut()
            fetch_mem(0)
            added(1, 1)
            for i in range(1, 4):
                fetch_mem(i)
            act.wait_ge(sems["mem_in"], 64)
            with w.loop(KD // 2 - 2, w_hi=8, cut=8, mem_hi_done=2, proj_read=2, block=2, square_done=2,
                        **{"square_read:free": 2}) as i:
                for k in range(2):
                    mem_high(i * 2 + k)
                    cut(4)
                    added(i * 2 + (k + 2), k)
            for k in range(2):
                m = KD - 2 + k
                mem_high(2 * m - KD)
                mem_high(2 * m - KD + 1)
                cut(4)
                added(m, k)

            MEMC = slice(0, M)

            def high_tiles(first, last):
                for k in range(first, last):
                    high_tile(k, "g_cross")
                    cut()

            cut(4)
            root(rmem[:, :])
            cut(4)
            high(kc_hi[:, 0, :], cols=MEMC)
            high(kc_hi[:, 1, :], cols=MEMC)
            high_tiles(0, 4)
            high(kc_hi[:, 2, :], cols=MEMC)
            cut(3)
            high(kc_hi[:, 3, :], cols=MEMC)
            high_tiles(4, 10)
            root(rstd[:, :])
            high_tiles(10, KD)
            cut(5)
            w.at["logits_read"] = Count(HEADS * QT)
            for t in range(MT):
                act.wait_ge(sems["logits_read"], w.next("logits_read"))
                copy(vc_hi[:, t, :], stage[:, t, :]).then_inc(sems["v_hi_done"], w.add("v_hi_done"))

            XPARTS = [xprob[:, t, :] for t in range(QT)]
            XLOGITS = [pair[t // 2][:, (t % 2) * M:(t % 2 + 1) * M] for t in range(QT)]
            XTURNED = [(xpt_hi[:, b, :], T) for b in range(MT)]
            for i in range(XH + 2):
                if i < XH:
                    cut()
                if 1 <= i <= XH:
                    exps(XPARTS, XLOGITS)
                if i < XH:
                    cut()
                if i >= 2:
                    attn_high(oc_hi[:, i - 2, :])
                if i < XH:
                    cut(2)
                    high(xq_hi[:, :])
                if 1 <= i <= XH:
                    turned_high(XTURNED)
            with w.loop(4, w_hi=4, cut=4, proj_read=4, block=4, act_hi_done=4, square_done=4, **{"square_read:free": 4}) as i:
                for k in range(4):
                    cut()
                    staged()
                    high_tile(i * 4 + k, "g_ffn")
                    square(i * 4 + k, k)

            def up_block(p, which):
                staged()
                blk = p + FB * which
                act.wait_ge(sems["ones_set"], 1)
                nc.scalar.activation(conv[:, which, :], padded[:, which, 2:T + 2], ACT.Identity,
                                     scale=col("conv_w", blk * 3 + 2), bias=col("conv_b", blk)).then_inc(
                                         sems["conv_in"], w.add("conv_in"))
                act.wait_ge(sems["conv_done"], w.next("conv_done"))

            def up(p, h_slot, before=None):
                cut(4)
                early = 0
                if before:
                    before()
                    early = 3
                cut(early)
                up_block(p, 0)
                nc.scalar.activation(sigm[:, :], conv[:, 0, :], ACT.Silu).then_inc(sems["silu_done"], w.add("silu_done"))
                cut(4 - early)
                up_block(p, 1)
                act.wait_ge(sems["h_ready"], w.next("h_ready"))
                act.wait_ge(sems["ones_set"], 1)
                copy(at(h_hi, h_slot), conv[:, 0, :]).then_inc(sems["h_hi_done"], w.add("h_hi_done"))

            PAIR = dict(w_hi=8, cut=8, proj_read=2, block=2, conv_in=2, conv_done=2, silu_done=1, h_ready=1, h_hi_done=1)
            up(0, 0, lambda: root(rstd[:, :]))
            with w.loop(CH - 1, **PAIR) as i:
                up(i + 1, i + 1)
            n = 16 * CH + 2 * 16
            with w.loop((NCH - 1) // 2, w_hi=n, cut=n, proj_read=4 * CH + 32, block=4 * CH + 32, conv_in=4 * CH,
                        conv_done=4 * CH, silu_done=2 * CH, h_ready=2 * CH, h_hi_done=2 * CH) as c:
                for part in range(2):
                    first = c * (2 * CH) + CH * (part + 1)
                    h0 = CH * (1 - part)
                    up(first, h0)
                    with w.loop(4, w_hi=4, cut=4, proj_read=4, block=4):
                        cut(4)
                        skip(4)
                    with w.loop(CH - 1, **PAIR) as i:
                        up(first + i + 1, i + (h0 + 1))

            def last_block(m, k):
                staged()
                square(m, k)

            with w.loop(3, w_hi=4, cut=4, proj_read=4, block=4, square_done=4, **{"square_read:free": 4}) as i:
                for k in range(4):
                    cut()
                    last_block(i * 4 + k, k)
            for k in range(12, KD):
                last_block(k, k)

            for m in P_TILES:
                nc.scalar.activation(res[:, m, :], res[:, m, :], ACT.Copy, scale=col("g_final", m)).then_inc(
                    sems["gained"], w.add("gained"))
            root(rstd[:, :])
            for m in P_TILES:
                act.wait_ge(sems["scaled_p"], w.next("scaled_p"))
                act.dma_start(out[:, m, :], res[:, m, :]).then_inc(sems["out_stored"], 16)

        @block.gpsimd
        def _(pool):
            w = Tally(pool)

            def tt(out_, a, b, op):
                return nc.gpsimd.tensor_tensor(out_, a, b, op)

            def step(ins):
                ins.then_inc(sems["pool_step"], w.add("pool_step"))
                pool.wait_ge(sems["pool_step"], w.value("pool_step"))

            def cut(k=1):
                for _ in range(k):
                    slot = w.now("cut").const % RING
                    pool.wait_ge(sems["w_hi"], w.next("w_hi"))
                    tt(wlo[:, slot, :], raw[:, slot, :], whi[:, slot, :].bitcast(F32), ALU.subtract).then_inc(
                        sems["w_lo"], w.add("w_lo"))
                    w.move("cut")

            def add_square(k):
                pool.wait_ge(sems["square_done"], w.next("square_done"))
                tt(sumsq[:, :], sumsq[:, :], sq[:, k, :], ALU.add).then_inc(sems["square_read"], w.add("square_read"))
                pool.wait_ge(sems["square_read"], w.value("square_read"))

            def add_squares(tiles):
                step(nc.gpsimd.memset(sumsq[:, :], 0.0))
                with w.loop(tiles // 2, square_done=2, square_read=2):
                    for k in range(2):
                        add_square(k)

            for dst, src in ((s5t[:, 0, :], b_re), (s5t[:, 1, :], b_im), (cc_re[:, :, :].rearrange("p j c -> p (j c)"), c_re),
                             (cc_im[:, :, :].rearrange("p j c -> p (j c)"), c_im),
                             (rel_sb[0:BUCKETS, :], rel), (onehot_sb[0:BUCKETS, :], onehot)):
                pool.dma_start(dst, src).then_inc(sems["s5_in"], 16)
            w.at["square_done"] = w.at["square_read"] = Count(KD)

            pool.wait_ge(sems["s5_sines"], w.next("s5_sines", 2))

            def doubled(c, s, levels):
                step(nc.gpsimd.memset(c[:, :, 0:1], 1.0))
                step(nc.gpsimd.memset(s[:, :, 0:1], 0.0))
                for v in range(levels):
                    n = 1 << v
                    shape = [P, ST, n]
                    pr, pi = (s5p[:, j, :].unsqueeze(2).to_broadcast(shape) for j in (6, 5))
                    t = s5q[:, 0:ST * n].rearrange("p (j n) -> p j n", n=n)
                    a, b, c2, s2 = c[:, :, 0:n], s[:, :, 0:n], c[:, :, n:2 * n], s[:, :, n:2 * n]
                    step(tt(c2, a, pr, ALU.mult))
                    step(tt(t, b, pi, ALU.mult))
                    step(tt(c2, c2, t, ALU.subtract))
                    step(tt(s2, a, pi, ALU.mult))
                    step(tt(t, b, pr, ALU.mult))
                    step(tt(s2, s2, t, ALU.add))
                    pr, pi, t0, t1 = s5p[:, 6, :], s5p[:, 5, :], s5p[:, 22, :], s5p[:, 23, :]
                    step(tt(t0, pi, pi, ALU.mult))
                    step(tt(t1, pr, pi, ALU.mult))
                    step(tt(pr, pr, pr, ALU.mult))
                    step(tt(pr, pr, t0, ALU.subtract))
                    step(tt(pi, t1, t1, ALU.add))

            pool.wait_ge(sems["s5_padded"], 1)
            doubled(tab_c, tab_s, FLO.bit_length() - 1)
            doubled(hop_c, hop_s, FHI.bit_length() - 1)
            nc.gpsimd.memset(s5q[:, 0:1], 0.0).then_inc(sems["s5_tables"], w.add("s5_tables"))

            def strip_load(h):
                src = bass.AP(tensor=strips.tensor, offset=h * P * (SPAN + 1) + P - 1, ap=[[SPAN, P], [1, T]])
                pool.dma_start(strip[:, :], src).then_inc(sems["strip_in"], 16)

            w.at["cut"] = w.at["w_hi"] = w.at["w_lo"] = Count(FIRST_POOL_CUT)
            pool.wait_ge(sems["w_lo"], w.value("w_lo"))
            pool.wait_ge(sems["strip_out"], 16)
            strip_load(0)
            with w.loop(6, w_hi=4, w_lo=4, cut=4):
                cut(4)

            def bias_and_mask(h):
                pool.wait_ge(sems["strip_in"], w.next("strip_in", 16))
                if w.due("logits_read:free", QT):
                    pool.wait_ge(sems["logits_read"], w.value("logits_read:free"))
                for t in range(QT):
                    ins = tt(biasm[:, OFF[t]:OFF[t] + KEYS[t]], strip[:, T - KEYS[t]:T], mask[:, OFF[t]:OFF[t] + KEYS[t]], ALU.add)
                    if t < QT - 1:
                        ins.then_inc(sems["pool_step"], w.add("pool_step"))
                ins.then_inc(sems["biasm_done"], w.add("biasm_done"))
                pool.wait_ge(sems["biasm_done"], w.value("biasm_done"))
                pool.wait_ge(sems["pool_step"], w.value("pool_step"))

            w.at["logits_read:free"] = Count(-QT)
            for i in range(HEADS):
                cut(2 if i else 4)
                if i == 0:
                    pool.wait_ge(sems["mask_done"], w.next("mask_done"))
                bias_and_mask(i)
                if i + 1 < HEADS:
                    strip_load(i + 1)
                cut(2 if i else 0)
            with w.loop((UNITS_BEFORE_OUT + 4 - FIRST_POOL_CUT - 24 - HEADS * 4) // 4, w_hi=4, w_lo=4, cut=4):
                cut(4)

            step(nc.gpsimd.memset(sumsq[:, :], 0.0))
            with w.loop(KD // 2, w_hi=8, w_lo=8, cut=8, square_done=2, square_read=2):
                for k in range(2):
                    cut(4)
                    add_square(k)
            with w.loop((LAST_POOL_CUT - UNITS_BEFORE_OUT - 4 - KD * UNITS_D) // 4, w_hi=4, w_lo=4, cut=4):
                cut(4)
            assert w.now("cut").const == LAST_POOL_CUT

            for tiles in (KD, KD - LAST_SQUARES):
                pool.wait_ge(sems["sumsq_total"], w.next("sumsq_total"))
                add_squares(tiles)
            pool.wait_ge(sems["newton_done"], w.next("newton_done"))
            for m in P_TILES:
                pool.wait_ge(sems["gained"], w.next("gained"))
                tt(res[:, m, :], res[:, m, :], rstd[:, :], ALU.mult).then_inc(sems["scaled_p"], w.add("scaled_p"))


def t5_buckets():
    n = np.maximum(T - 1 - np.arange(SPAN), 0)
    exact = BUCKETS // 2
    nf = np.maximum(n, 1).astype(np.float32)
    large = exact + (np.log(nf / np.float32(exact)) / np.float32(np.log(128 / exact))
                     * np.float32(BUCKETS - exact)).astype(np.int32)
    return np.where(n < exact, n, np.minimum(large, BUCKETS - 1))


def units(wt):
    k, m = wt.shape
    return wt.reshape(k // T, UT, P, m // P, P).transpose(3, 0, 2, 1, 4).reshape(m // P, k // T, P, T)


def columns(v):
    return np.asarray(v).reshape(-1, P).T


def weight_stream(w_in, w_glu, w_a, w_b, w_out, w_q, w_kv, w_o, w_up, w_down):
    parts = []

    def put(a):
        parts.append(a.reshape(-1, P, T))

    cuts = np.cumsum([HEADS * DH, KVH * DH, KVH * DH, IH * ID, ID, IH, SSM, D, D])
    q, k, v, qi, ki, wi, s, ga, gb = np.split(w_in, cuts[:-1], axis=1)
    put(units(np.concatenate([ki, wi, np.zeros((D, P - ID - IH), np.float32)], axis=1)))
    for m in (qi, k, v):
        put(units(m))
    s = units(s)
    put(s[2:4])
    put(units(q))
    put(s[0:2])
    ga, a, gb, b = units(ga), units(w_a), units(gb), units(w_b)
    for m in range(KD):
        put(ga[m])
        put(a[m])
    put(gb[0:8])
    put(units(w_glu))
    put(gb[8:16])
    put(b)
    put(units(w_out))
    put(units(w_kv[:, :XH * P]))
    put(w_kv[:, XH * P:])
    put(units(w_q))
    put(units(w_o))
    up, down = units(w_up), w_down
    for c in range(NCH + 1):
        for p in range(CH):
            if c < NCH:
                put(up[c * CH + p])
                put(up[FB + c * CH + p])
            if p == 0 and c > 0:
                put(units(down[(c - 1) * CH * P:c * CH * P]))
    return np.concatenate(parts, axis=0)


def kernel(**inputs):
    import concourse.bacc as bacc
    from concourse.bass_utils import run_bass_kernel_spmd

    a = {n: np.asarray(v) for n, v in inputs.items()}
    one = {n: v[0] for n, v in a.items() if n not in ("rel_bias", "norm_final")}

    def feature_major(x):
        return x.T.reshape(KD, P, x.shape[0]).transpose(1, 0, 2)

    def per_state(v):
        return v.reshape(ST, P).T

    def block_diagonal(m):
        z = np.zeros((ST, 2, GP, 2, GC), np.float32)
        m = m.reshape(ST, 2, GP, GC)
        for g in range(2):
            z[:, g, :, g, :] = m[:, g]
        return z.reshape(ST, P, 2 * GC).transpose(1, 0, 2).reshape(P, ST * 2 * GC)

    conv_w = one["ffn_conv_w"].reshape(3, 2 * FB, P).transpose(2, 1, 0).reshape(P, 6 * FB)
    pieces = {
        "g_mix": columns(one["norm_mix"]), "g_cross": columns(one["norm_cross"]), "g_mem": columns(one["norm_mem"]),
        "g_ffn": columns(one["norm_ffn"]), "g_final": columns(a["norm_final"]), "ident": np.eye(P, dtype=np.float32),
        "causal": np.where(np.arange(P)[None, :] > np.arange(P)[:, None], np.float32(NEG), np.float32(0)),
        "lam_re": per_state(one["ssm_lambda_re"]), "lam_im": per_state(one["ssm_lambda_im"]),
        "log_dt": per_state(np.repeat(one["ssm_log_dt"], GP)), "b_glu": columns(one["ssm_b_glu"]),
        "d_skip": columns(one["ssm_d"].reshape(-1)), "conv_b": columns(one["ffn_conv_b"]), "conv_w": conv_w,
    }
    onehot = (t5_buckets()[None, :] == np.arange(BUCKETS)[:, None]).astype(np.float32)
    arrays = {
        "wstream": weight_stream(one["w_in"], one["ssm_w_glu"], one["w_branch_a"], one["w_branch_b"], one["w_out"],
                                 one["w_cross_q"], one["w_cross_kv"], one["w_cross_o"], one["w_up"], one["w_down"]),
        "xt": feature_major(one["x"]),
        "memt": feature_major(one["mem"]),
        "params": np.concatenate([pieces[n] for n, _ in PARAMS], axis=1),
        "b_re": block_diagonal(one["ssm_b_re"]), "b_im": block_diagonal(one["ssm_b_im"]),
        "c_re": block_diagonal(one["ssm_c_re"].transpose(0, 2, 1)), "c_im": block_diagonal(one["ssm_c_im"].transpose(0, 2, 1)),
        "rel": a["rel_bias"], "onehot": onehot,
    }
    arrays = {n: np.ascontiguousarray(v) for n, v in arrays.items()}
    nc = bacc.Bacc("TRN2", target_bir_lowering=False, num_devices=1)
    args = [nc.dram_tensor(n, v.shape, mybir.dt.from_np(v.dtype), kind="ExternalInput").ap() for n, v in arrays.items()]
    strips = nc.dram_tensor("strips", (HEADS, P, SPAN + 1), F32, kind="Internal").ap()
    out = nc.dram_tensor("out", (P, KD, T), F32, kind="ExternalOutput").ap()
    layer(nc, *args, strips, out)
    got = run_bass_kernel_spmd(nc, [arrays], core_ids=[0]).results[0]["out"]
    return got.transpose(1, 0, 2).reshape(D, T).T[None]
```
